# Optimizing a Trainium2 kernel written in Bass

```python
import jax, jax.numpy as jnp
from jax import lax
import numpy as np

D_MODEL = 2048
BATCH = 1
SEQ = 512
DEPTH = 1
DEC_BATCH = 1
DEC_SEQ = 64
PAST_LEN = 512

CHUNK = 64
HEAD_DIM = 128
D_A = D_MODEL // 2
N_BLOCKS_A = D_A // HEAD_DIM
H_B = D_MODEL // 4 // HEAD_DIM
H_C = D_MODEL // 4 // HEAD_DIM
D_B = H_B * HEAD_DIM
D_C = H_C * HEAD_DIM
D_MIX = D_A + D_B + D_C
CONV_W = 4
LRU_C = 8.0
N_PREV_CHUNKS = 8
BAND = N_PREV_CHUNKS * CHUNK
REL_CLIP = 256
N_REL = 2 * REL_CLIP + 1
D_FF = 4 * D_MODEL
D_IN = 2 * D_A + 3 * D_B + 3 * D_C + H_C
SPLITS = (D_A, 2 * D_A, 2 * D_A + D_B, 2 * D_A + 2 * D_B, 2 * D_A + 3 * D_B,
          2 * D_A + 3 * D_B + D_C, 2 * D_A + 3 * D_B + 2 * D_C, 2 * D_A + 3 * D_B + 3 * D_C)
ALPHA = (2 * DEPTH) ** 0.25
BETA = (8 * DEPTH) ** -0.25
Q_BLOCK = 128
SCALE = HEAD_DIM ** -0.5
LN_EPS = 1e-5
NEG = -1e30

kernel_name = "hybrid_streaming_encoder_step"

def _layer_norm(x, g, b):
    xf = x.astype(jnp.float32)
    mu = jnp.mean(xf, -1, keepdims=True)
    var = jnp.mean(jnp.square(xf - mu), -1, keepdims=True)
    return ((xf - mu) * lax.rsqrt(var + LN_EPS) * g + b).astype(x.dtype)

def _rms_norm(x, g):
    xf = x.astype(jnp.float32)
    return (xf * lax.rsqrt(jnp.mean(xf * xf, -1, keepdims=True) + LN_EPS) * g).astype(x.dtype)

def _project(x, w_in, b_forget):
    B, T = x.shape[:2]
    a_x, a_g, bq, bk, bv, cq, ck, cv, cf = jnp.split(jnp.einsum('btd,de->bte', x, w_in), SPLITS, axis=-1)
    heads = lambda t, n: t.reshape(B, T, n, HEAD_DIM)
    logf = jax.nn.log_sigmoid((cf + b_forget).astype(jnp.float32))
    return (a_x, a_g, heads(bq, H_B), heads(bk, H_B), heads(bv, H_B),
            heads(cq, H_C), heads(ck, H_C), heads(cv, H_C), logf)

def _lin_combine(c1, c2):
    a1, b1 = c1
    a2, b2 = c2
    return a1 * a2, a2 * b1 + b2

def _rglru(xa, conv_buf, h0, w_conv, b_conv, w_ra, b_ra, w_rx, b_rx, lam, reset_first):
    B, T, _ = xa.shape
    xe = jnp.concatenate([conv_buf.astype(xa.dtype), xa], axis=1)
    xc = b_conv + sum(w_conv[j] * xe[:, j:j + T] for j in range(CONV_W))
    xb = xc.reshape(B, T, N_BLOCKS_A, HEAD_DIM)
    r = jax.nn.sigmoid(jnp.einsum('btnd,nde->btne', xb, w_ra).reshape(B, T, D_A) + b_ra)
    i = jax.nn.sigmoid(jnp.einsum('btnd,nde->btne', xb, w_rx).reshape(B, T, D_A) + b_rx)
    log_a = -LRU_C * r.astype(jnp.float32) * jax.nn.softplus(-lam.astype(jnp.float32))
    a = jnp.exp(log_a)
    mult = jnp.sqrt(-jnp.expm1(2.0 * log_a))
    if reset_first:
        mult = mult.at[:, 0].set(1.0)
    u = mult * (i * xc).astype(jnp.float32)
    u = u.at[:, 0].add(a[:, 0] * h0.astype(jnp.float32))
    _, h = lax.associative_scan(_lin_combine, (a, u), axis=1)
    return h, xe[:, -(CONV_W - 1):], h[:, -1]

def _rel_bias(table, dist):
    return table[:, jnp.clip(dist, -REL_CLIP, REL_CLIP) + REL_CLIP].astype(jnp.float32)

def _band_prompt(q, k, v, rel_table):
    B, S = q.shape[:2]
    nc = S // CHUNK
    nk = (N_PREV_CHUNKS + 1) * CHUNK
    qc = q.reshape(B, nc, CHUNK, H_B, HEAD_DIM)
    pad = jnp.zeros((B, N_PREV_CHUNKS, CHUNK, H_B, HEAD_DIM), k.dtype)
    kp = jnp.concatenate([pad, k.reshape(B, nc, CHUNK, H_B, HEAD_DIM)], axis=1)
    vp = jnp.concatenate([pad, v.reshape(B, nc, CHUNK, H_B, HEAD_DIM)], axis=1)
    kband = jnp.concatenate([kp[:, j:j + nc] for j in range(N_PREV_CHUNKS + 1)], axis=2)
    vband = jnp.concatenate([vp[:, j:j + nc] for j in range(N_PREV_CHUNKS + 1)], axis=2)
    qi = jnp.arange(CHUNK)[:, None]
    km = jnp.arange(nk)[None, :]
    bias = _rel_bias(rel_table, BAND + qi - km)
    valid = (jnp.arange(nc)[:, None] * CHUNK - BAND + jnp.arange(nk)[None, :]) >= 0
    s = jnp.einsum('bnqhd,bnkhd->bnhqk', qc, kband).astype(jnp.float32) * SCALE + bias[None, None]
    s = jnp.where(valid[None, :, None, None, :], s, NEG)
    p = jax.nn.softmax(s, axis=-1).astype(v.dtype)
    o = jnp.einsum('bnhqk,bnkhd->bnqhd', p, vband)
    return o.reshape(B, S, D_B)

def _band_sample(q, k_new, v_new, k_cache, v_cache, rel_table):
    B, T = q.shape[:2]
    n_c = k_cache.shape[1]
    k = jnp.concatenate([k_cache.astype(k_new.dtype), k_new], axis=1)
    v = jnp.concatenate([v_cache.astype(v_new.dtype), v_new], axis=1)
    pos_k = jnp.concatenate([jnp.arange(n_c) - n_c, jnp.arange(T)])
    bias = _rel_bias(rel_table, jnp.arange(T)[:, None] - pos_k[None, :])
    s = jnp.einsum('bqhd,bkhd->bhqk', q, k).astype(jnp.float32) * SCALE + bias[None]
    p = jax.nn.softmax(s, axis=-1).astype(v.dtype)
    return jnp.einsum('bhqk,bkhd->bqhd', p, v).reshape(B, T, D_C)

def _fox_attend(q, fq, tq, k, v, fk, tk):
    s = jnp.einsum('bqhd,bkhd->bhqk', q, k).astype(jnp.float32) * SCALE
    s = s + (jnp.swapaxes(fq, 1, 2)[..., :, None] - jnp.swapaxes(fk, 1, 2)[..., None, :])
    s = jnp.where(tk[None, :] <= tq[:, None], s, NEG)
    p = jax.nn.softmax(s, axis=-1).astype(v.dtype)
    return jnp.einsum('bhqk,bkhd->bqhd', p, v)

def _fox_prompt(q, k, v, logf):
    B, S = q.shape[:2]
    F = jnp.cumsum(logf.astype(jnp.float32), axis=1)
    nb = S // Q_BLOCK
    qb = q.reshape(B, nb, Q_BLOCK, H_C, HEAD_DIM).transpose(1, 0, 2, 3, 4)
    fb = F.reshape(B, nb, Q_BLOCK, H_C).transpose(1, 0, 2, 3)
    tq = jnp.arange(S).reshape(nb, Q_BLOCK)
    tk = jnp.arange(S)
    o = lax.map(lambda blk: _fox_attend(blk[0], blk[1], blk[2], k, v, F, tk), (qb, fb, tq))
    return o.transpose(1, 0, 2, 3, 4).reshape(B, S, D_C)

def _fox_sample(q, k_new, v_new, logf_new, k_cache, v_cache, logf_cache):
    B, T = q.shape[:2]
    P = k_cache.shape[1]
    k = jnp.concatenate([k_cache.astype(k_new.dtype), k_new], axis=1)
    v = jnp.concatenate([v_cache.astype(v_new.dtype), v_new], axis=1)
    F = jnp.cumsum(jnp.concatenate([logf_cache.astype(jnp.float32), logf_new], axis=1), axis=1)
    o = _fox_attend(q, F[:, P:], P + jnp.arange(T), k, v, F, jnp.arange(P + T))
    return o.reshape(B, T, D_C)

def _finish_layer(x, y_a, y_b, y_c, g_mix, w_out, ln1_g, ln1_b, w_up, w_down, ln2_g, ln2_b):
    y = jnp.concatenate([_rms_norm(y_a, g_mix[:D_A]),
                         _rms_norm(y_b, g_mix[D_A:D_A + D_B]),
                         _rms_norm(y_c, g_mix[D_A + D_B:])], axis=-1)
    x = _layer_norm(ALPHA * x + jnp.einsum('btm,md->btd', y, w_out), ln1_g, ln1_b)
    hdn = jnp.square(jax.nn.relu(jnp.einsum('btd,df->btf', x, w_up)))
    return _layer_norm(ALPHA * x + jnp.einsum('btf,fd->btd', hdn, w_down), ln2_g, ln2_b)

def setup_inputs(seed: int = 0) -> dict:
    key = jax.random.key(seed)
    ks = jax.random.split(key, 32)
    f32 = jnp.float32
    nrm = lambda k, shape, s: jax.random.normal(k, shape, f32) * s
    band_rows = min(BAND, PAST_LEN)
    u = jax.random.uniform(ks[15], (DEPTH, D_A), f32, minval=0.9, maxval=0.999)
    a_base = u ** (1.0 / LRU_C)
    lru_lambda = jnp.log(a_base) - jnp.log1p(-a_base)
    return {
        "x_prompt": nrm(ks[0], (BATCH, SEQ, D_MODEL), 1.0),
        "x_sample": nrm(ks[1], (DEC_BATCH, DEC_SEQ, D_MODEL), 1.0),
        "state_conv": nrm(ks[2], (DEPTH, DEC_BATCH, CONV_W - 1, D_A), 1.0),
        "state_lru": nrm(ks[3], (DEPTH, DEC_BATCH, D_A), 0.5),
        "cache_band_k": nrm(ks[4], (DEPTH, DEC_BATCH, band_rows, H_B, HEAD_DIM), 1.0),
        "cache_band_v": nrm(ks[5], (DEPTH, DEC_BATCH, band_rows, H_B, HEAD_DIM), 1.0),
        "cache_fox_k": nrm(ks[6], (DEPTH, DEC_BATCH, PAST_LEN, H_C, HEAD_DIM), 1.0),
        "cache_fox_v": nrm(ks[7], (DEPTH, DEC_BATCH, PAST_LEN, H_C, HEAD_DIM), 1.0),
        "cache_fox_logf": jax.nn.log_sigmoid(nrm(ks[8], (DEPTH, DEC_BATCH, PAST_LEN, H_C), 1.0) + 4.0),
        "w_in": nrm(ks[9], (DEPTH, D_MODEL, D_IN), D_MODEL ** -0.5),
        "w_conv": nrm(ks[10], (DEPTH, CONV_W, D_A), CONV_W ** -0.5),
        "b_conv": nrm(ks[11], (DEPTH, D_A), 0.02),
        "w_rg_a": nrm(ks[12], (DEPTH, N_BLOCKS_A, HEAD_DIM, HEAD_DIM), HEAD_DIM ** -0.5),
        "b_rg_a": nrm(ks[13], (DEPTH, D_A), 0.02),
        "w_rg_x": nrm(ks[14], (DEPTH, N_BLOCKS_A, HEAD_DIM, HEAD_DIM), HEAD_DIM ** -0.5),
        "b_rg_x": nrm(ks[16], (DEPTH, D_A), 0.02),
        "lru_lambda": lru_lambda,
        "rel_bias": nrm(ks[17], (DEPTH, H_B, N_REL), 0.2),
        "b_forget": jax.random.uniform(ks[18], (DEPTH, H_C), f32, minval=2.0, maxval=6.0),
        "g_mix": 1.0 + nrm(ks[19], (DEPTH, D_MIX), 0.02),
        "w_out": nrm(ks[20], (DEPTH, D_MIX, D_MODEL), BETA * D_MIX ** -0.5),
        "ln1_g": 1.0 + nrm(ks[21], (DEPTH, D_MODEL), 0.02),
        "ln1_b": nrm(ks[22], (DEPTH, D_MODEL), 0.02),
        "w_up": nrm(ks[23], (DEPTH, D_MODEL, D_FF), D_MODEL ** -0.5),
        "w_down": nrm(ks[24], (DEPTH, D_FF, D_MODEL), BETA * D_FF ** -0.5),
        "ln2_g": 1.0 + nrm(ks[25], (DEPTH, D_MODEL), 0.02),
        "ln2_b": nrm(ks[26], (DEPTH, D_MODEL), 0.02),
    }

def reference(x_prompt, x_sample, state_conv, state_lru, cache_band_k, cache_band_v,
              cache_fox_k, cache_fox_v, cache_fox_logf, w_in, w_conv, b_conv, w_rg_a, b_rg_a,
              w_rg_x, b_rg_x, lru_lambda, rel_bias, b_forget, g_mix, w_out, ln1_g, ln1_b,
              w_up, w_down, ln2_g, ln2_b):
    xp, xs = x_prompt, x_sample
    Bp, S = xp.shape[:2]
    n_band_p = min(BAND, S)
    p_conv, p_lru, p_bk, p_bv, p_fk, p_fv, p_fl = [], [], [], [], [], [], []
    s_conv, s_lru, s_bk, s_bv, s_fk, s_fv, s_fl = [], [], [], [], [], [], []
    for l in range(DEPTH):
        lru_w = (w_conv[l], b_conv[l], w_rg_a[l], b_rg_a[l], w_rg_x[l], b_rg_x[l], lru_lambda[l])
        out_w = (g_mix[l], w_out[l], ln1_g[l], ln1_b[l], w_up[l], w_down[l], ln2_g[l], ln2_b[l])

        a_x, a_g, bq, bk, bv, cq, ck, cv, logf = _project(xp, w_in[l], b_forget[l])
        h, buf, h_last = _rglru(a_x, jnp.zeros((Bp, CONV_W - 1, D_A), xp.dtype),
                                jnp.zeros((Bp, D_A), jnp.float32), *lru_w, reset_first=True)
        y_a = h.astype(xp.dtype) * jax.nn.gelu(a_g)
        y_b = _band_prompt(bq, bk, bv, rel_bias[l])
        y_c = _fox_prompt(cq, ck, cv, logf)
        xp = _finish_layer(xp, y_a, y_b, y_c, *out_w)
        p_conv.append(buf)
        p_lru.append(h_last)
        p_bk.append(bk[:, S - n_band_p:])
        p_bv.append(bv[:, S - n_band_p:])
        p_fk.append(ck)
        p_fv.append(cv)
        p_fl.append(logf)

        a_x, a_g, bq, bk, bv, cq, ck, cv, logf = _project(xs, w_in[l], b_forget[l])
        h, buf, h_last = _rglru(a_x, state_conv[l], state_lru[l], *lru_w, reset_first=False)
        y_a = h.astype(xs.dtype) * jax.nn.gelu(a_g)
        y_b = _band_sample(bq, bk, bv, cache_band_k[l], cache_band_v[l], rel_bias[l])
        y_c = _fox_sample(cq, ck, cv, logf, cache_fox_k[l], cache_fox_v[l], cache_fox_logf[l])
        xs = _finish_layer(xs, y_a, y_b, y_c, *out_w)
        s_conv.append(buf)
        s_lru.append(h_last)
        s_bk.append(bk)
        s_bv.append(bv)
        s_fk.append(ck)
        s_fv.append(cv)
        s_fl.append(logf)

    st = lambda xs_list: jnp.stack(xs_list, axis=0)
    return (xp, xs,
            st(p_conv), st(p_lru), st(p_bk), st(p_bv), st(p_fk), st(p_fv), st(p_fl),
            st(s_conv), st(s_lru), st(s_bk), st(s_bv), st(s_fk), st(s_fv), st(s_fl))


_drawn_inputs = setup_inputs


def setup_inputs(seed=0):
    import zlib

    import numpy as np

    out = dict(_drawn_inputs(seed))
    spreads = {}
    factors = {'cache_fox_logf': 3.941,
     'b_rg_a': 8.0,
     'b_rg_x': 7.335,
     'g_mix': 6.185,
     'ln1_b': 2.686,
     'ln2_g': 2.724,
     'ln2_b': 2.899}
    for name, (base, spread) in spreads.items():
        noise = np.random.default_rng([zlib.crc32(name.encode()), seed]).standard_normal(out[name].shape)
        drawn = base * np.exp(spread * noise) if base else spread * noise
        out[name] = __import__('jax').numpy.asarray(drawn.astype(out[name].dtype))
    for name, factor in factors.items():
        out[name] = (out[name] * factor).astype(out[name].dtype)
    return out
```

```python
import concourse.bass as bass
from concourse import mybir
from contextlib import ExitStack

F32, F32R = mybir.dt.float32, mybir.dt.float32r
ALU, ACT, AX = mybir.AluOpType, mybir.ActivationFunctionType, mybir.AxisListType

D, SEQ, DEC, PAST, HD, DA, DFF = 2048, 512, 64, 512, 128, 1024, 8192
TOK, HALF = SEQ + DEC, (SEQ + DEC) // 2
KT = D // 128
NA = DA // 128
NH = 4
CONV = 4
NREL, CLIP = 513, 256
D_IN = 2 * DA + 6 * NH * HD + NH
F_COL = D_IN - NH
ALPHA, SCALE, EPS, NEG = 2.0 ** 0.25, HD ** -0.5, 1e-5, -1e30
GELU0 = 0.7978845608028654
GELU1 = GELU0 * 0.044715
UK, UC = 8, 256

G_A = 0
G_B = G_A + 8
G_O = G_B + 12
G_F = G_O + 8
N_CHUNK, FT = 8, 8
XW = 584
CW = 580
S_AT = SEQ + CONV - 1
S_LEN = [128, 256, 384, SEQ, PAST + DEC]
S_OFF = [0, 128, 384, 768, 1280]
S_ALL = sum(S_LEN)
BW = 640
REV = BW - 1 - CLIP
EW = 768


def encoder_step(nc, x_prompt, x_sample, state_conv, state_lru, band_k, band_v, fox_k, fox_v, fox_logf,
                 w_in, w_conv, b_conv, w_ra, b_ra, w_rx, b_rx, lam, rel_bias, b_forget, g_mix, w_out,
                 ln1_g, ln1_b, w_up, w_down, ln2_g, ln2_b,
                 y_prompt, y_sample, p_conv, p_lru, p_bk, p_bv, p_fk, p_fv, p_fl,
                 s_conv, s_lru, s_bk, s_bv, s_fk, s_fv, s_fl):
    ctx = ExitStack()
    with ctx:
        def sb(name, shape, dt=F32):
            return ctx.enter_context(nc.sbuf_tensor(name, shape, dt))

        def sem(name):
            return ctx.enter_context(nc.semaphore(name))

        class Region:
            def __init__(self):
                self.stack = ExitStack()

            def sb(self, name, shape, dt=F32):
                return self.stack.enter_context(nc.sbuf_tensor(name, shape, dt))

            def close(self):
                self.stack.close()

        RAW = [sb(f"raw{s}", [128, UK, UC]) for s in range(2)]
        WH = [sb(f"w_hi{s}", [128, UK, UC], F32R) for s in range(2)]
        WL = [sb(f"w_lo{s}", [128, UK, UC], F32R) for s in range(2)]
        ident = sb("ident", [128, 128])
        ones = sb("ones", [128, 128])
        sel = sb("sel", [NH, NH, 128])
        VT1 = sb("vec1", [128, 128])
        VT2 = sb("vec2", [128, 48])
        half_b = sb("half_b", [128, 2, NA])
        c_sp = sb("c_sp", [128, 2, NA])
        last = sb("last", [128, 64])
        LROW = sb("last_rows", [64, 128])
        eps = sb("eps", [128, 1])
        tiny = sb("tiny", [128, 8])
        small = sb("small", [128, 5, 3])
        LFT = sb("logf_rows", [128, 5, NH])
        FQ = sb("f_rows", [128, 5, NH])
        GM, L1G, L1B, L2G, L2B = (VT1[:, 16 * i:16 * i + 16] for i in range(5))
        WC, BC = VT1[:, 80:112], VT1[:, 112:120]
        H0, SC = VT2[:, 16:24], VT2[:, 24:48]

        r = Region()
        M = r.sb("band_bias", [128, NH, BW])
        r.close()
        r = Region()
        BF = r.sb("fox_bias", [128, S_ALL])
        r.close()
        r = Region()
        N0, N1, N2, N3 = (r.sb(f"norm{i}", [128, TOK]) for i in range(4))
        r.close()
        r = Region()
        RT = [r.sb(f"relu{m}", [128, TOK]) for m in range(2)]
        r.close()
        sb("extra", [128, NH * BW])
        r = Region()
        XL = r.sb("x_lo", [128, KT, TOK], F32R)
        r.close()
        r = Region()
        X1L = r.sb("x1_lo", [128, KT, TOK], F32R)
        r.close()
        R = sb("resid", [128, KT, TOK])
        r = Region()
        XH = r.sb("x_hi", [128, KT, TOK], F32R)
        r.close()
        r = Region()
        YH = r.sb("y_hi", [128, KT, TOK], F32R)
        r.close()
        r = Region()
        X1H = r.sb("x1_hi", [128, KT, TOK], F32R)
        r.close()
        r = Region()
        OUT = [r.sb(f"out_rows{i}", [128, D]) for i in range(2)]
        r.close()
        r = Region()
        FB = r.sb("f_prompt", [128, NH, SEQ])
        FSB = r.sb("f_sample", [128, NH, PAST + DEC])
        S = r.sb("scores", [128, S_ALL])
        PT = r.sb("probs_t", [128, 4, SEQ])
        PTS = r.sb("probs_t_s", [128, 5, DEC])
        r.close()
        sb("region_x", [128, KT * TOK])
        r = Region()
        XROW = r.sb("x_rows", [128, 4, D])
        VR1 = r.sb("vec_rows1", [128, 128])
        VR2 = r.sb("vec_rows2", [48, 128])
        CFL = r.sb("cache_logf", [128, 4, NH])
        r.close()
        r = Region()
        YF = r.sb("y_f32", [128, KT, TOK])
        r.close()
        r = Region()
        r.sb("gates", [128, NA * TOK])
        STG = r.sb("stage", [128, 2, TOK])
        GI = r.sb("gelu_in", [128, TOK])
        TH = r.sb("gelu_tanh", [128, TOK])
        GG = r.sb("gelu_gg", [128, TOK])
        FP = r.sb("f_cum_prompt", [NH, TOK])
        FS = r.sb("f_cum_sample", [NH, PAST + DEC])
        SSA = r.sb("ss_a", [128, TOK])
        r.close()
        ACC = sb("acc", [128, KT, TOK])
        r = Region()
        XROWS = r.sb("x_rows_s", [DEC, D])
        REL = r.sb("rel_table", [NH, NREL])
        EXT = r.sb("rel_reversed", [NH, EW])
        r.sb("x_lo_gap", [128, NA * XW - D - NREL - EW])
        ZT, ZA, ZB, ZC = (r.sb(n, [NH, TOK]) for n in ("z", "za", "zb", "zc"))
        CL = r.sb("cache_logf_t", [NH, PAST])
        LZ = r.sb("lz", [128, 4, NA])
        r.close()
        r = Region()
        XA = r.sb("conv_in", [128, NA, XW])
        XC, TR, TI, AA, T1, UX, HS = (r.sb(n, [128, CW]) for n in ("xc", "tr", "ti", "a", "t1", "u", "h"))
        WRA, WRX = (r.sb(n, [128, HD]) for n in ("w_ra", "w_rx"))
        r.close()
        r = Region()
        QF, KF, VF = ([r.sb(f"{n}{i}", [128, TOK]) for i in range(2)] for n in "qkv")
        KC, VC = ([r.sb(f"{n}c{i}", [128, 4, HD]) for i in range(2)] for n in "kv")
        KCT = r.sb("kct", [128, PAST])
        VT, KTM = ([r.sb(f"{n}t{i}", [128, 5, HD]) for i in range(2)] for n in "vk")
        r.close()
        r = Region()
        YL = r.sb("y_lo", [128, KT, TOK], F32R)
        r.close()
        r = Region()
        HHI = r.sb("h_hi", [128, FT, TOK], F32R)
        HLO = r.sb("h_lo", [128, FT, TOK], F32R)
        r.close()
        sb("region_h", [128, KT * TOK])
        PS = ctx.enter_context(nc.psum_tensor("psum", [128, 8, 512], F32))
        PSF = PS[:, :, :].rearrange("p b c -> p (b c)")
        QS = nc.dram_tensor("qkv_scratch", [6 * NH, 128, TOK], F32).ap()
        EXD = nc.dram_tensor("rel_reversed_dram", [NH, EW], F32).ap()
        REP = nc.dram_tensor("rel_repeated", [NH, 128, EW], F32).ap()

        raw_in = [sem(f"raw_in{s}") for s in range(2)]
        hi_done, lo_done = sem("hi_done"), sem("lo_done")
        unit_done = sem("unit_done")
        m0_done = sem("m0_done")
        ev = [sem(f"evacuated{m}") for m in range(2)]
        x_in, vec_in, cf_clear = sem("x_in"), sem("vec_in"), sem("cf_clear")
        const_done, vec_t, vec_done = sem("const_done"), sem("vec_t"), sem("vec_done")
        xt_done, xh_done, xl_done = sem("xt_done"), sem("xh_done"), sem("xl_done")
        rel_in, ext_done, ext_out, rep_out = sem("rel_in"), sem("ext_done"), sem("ext_out"), sem("rep_out")
        m_in, m_done, pool_m = sem("m_in"), sem("m_done"), sem("pool_m")
        act_c, dve_c, pool_c = sem("act_chain"), sem("dve_chain"), sem("pool_chain")
        z_abs, z_exp, z_u, z_ln, z_fwd = sem("z_abs"), sem("z_exp"), sem("z_u"), sem("z_ln"), sem("z_fwd")
        f_done, ft_done, ftc_done = sem("f_done"), sem("ft_done"), sem("ftc_done")
        xa_init, last_a = sem("xa_init"), sem("last_a")
        gw_in, conv_done, gate_done = sem("gate_w_in"), sem("conv_done"), sem("gate_done")
        a_done, ti_done, th_done, gi_done = sem("a_done"), sem("ti_done"), sem("th_done"), sem("gi_done")
        a2_done, m2_done, sq_done, sq_fix = sem("a2_done"), sem("m2_done"), sem("sq_done"), sem("sq_fix")
        scan_done, y_done, ss_done = sem("scan_done"), sem("y_done"), sem("ss_done")
        stg_done = sem("stg_done")
        stg_out = [sem(f"stg_out{m}") for m in range(2)]
        r_alpha, r_init = sem("r_alpha"), sem("r_init")
        ssa_mm, ssa_sd, ssa_rs, ya_done = sem("ssa_mm"), sem("ssa_sd"), sem("ssa_rs"), sem("ya_done")
        fb_mm, fb_done = sem("fb_mm"), sem("fb_done")
        att_in = [sem(f"att_in{i}") for i in range(2)]
        kv_out = [sem(f"kv_out{i}") for i in range(2)]
        tp, tc, sc, mx, ex, pn = (sem(n) for n in ("tp", "tc", "sc", "mx", "ex", "pn"))
        pt, ptc, bf_done = sem("pt"), sem("ptc"), sem("bf_done")
        pv_done, yv = sem("pv_done"), sem("yv")
        ysq, yss, y_mm, y_sd, y_rs, y_g = (sem(n) for n in ("ysq", "yss", "y_mm", "y_sd", "y_rs", "y_g"))
        yh_done, y_ready = sem("yh_done"), sem("y_ready")
        r_done = sem("r_done")
        x1h_done, acc_init, x1_ready = sem("x1h_done"), sem("acc_init"), sem("x1_ready")
        hh_done, h_ready, acc_done = sem("hh_done"), sem("h_ready"), sem("acc_done")
        settled = sem("settled")
        last_t, last_c = sem("last_t"), sem("last_c")
        out_t, out_c, stores = sem("out_t"), sem("out_c"), sem("stores")
        out_rows = [sem(f"out_rows{i}") for i in range(2)]

        class NormSems:
            def __init__(self, n):
                self.s1, self.mm1, self.mean, self.xc, self.sq, self.s2, self.mm2, self.sd, self.rs, self.g, self.b = (
                    sem(f"{n}_{w}") for w in ("sum", "mm1", "mean", "centred", "sq", "sumsq", "mm2", "sd", "rstd",
                                              "scaled", "shifted"))

        n1, n2 = NormSems("ln1"), NormSems("ln2")

        class Chain:
            def __init__(self, eng, s):
                self.eng, self.s, self.n, self.base, self.stack = eng, s, 0, 0, []

            def __call__(self, ins):
                ins.then_inc(self.s, 1)
                self.n += 1
                self.eng.wait_ge(self.s, self.base + self.n)

            def enter(self, i, per, times):
                self.stack.append((self.n, self.base, per, times))
                self.base, self.n = i * per + (self.base + self.n), 0

            def leave(self):
                n, base, per, times = self.stack.pop()
                assert self.n == per, (self.n, per)
                self.n, self.base = n + per * times, base

        def one(t, k):
            return t[:, bass.ds(k, 1), :].rearrange("p a c -> p (a c)")

        def settle(eng):
            eng.sem_inc(settled, 1)

        def flat(t):
            return t[:, :, :].rearrange("p k c -> p (k c)")

        def one_dram(t, k):
            return t[bass.ds(k, 1), :, :].rearrange("a p c -> (a p) c")

        def cache_head(t, h):
            return t.rearrange("(j p) h d -> p j h d", p=128)[:, :, bass.ds(h, 1), :].rearrange("p j a d -> p j (a d)")

        def row_head(t, h):
            return t[:, bass.ds(h, 1), :].rearrange("t a d -> t (a d)")

        def tile_s(i, n):
            return S[0:n, S_OFF[i]:S_OFF[i] + S_LEN[i]]

        def gate2(t):
            return t[:, :].rearrange("p (h c) -> p h c", h=2)

        def done(m, G, Mc):
            return (unit_done, G * 2 + 4) if m else (m0_done, Mc + 1)

        def done_down(m, s, c, j):
            return (unit_done, c * 16 + j * 2 + (2 * (G_F + 4) + 3 + s)) if m \
                else (m0_done, c * 12 + j * 2 + (G_F + 4 + s + 1))

        def pair(m, rows=128):
            return PS[0:rows, 2 * m:2 * m + 2, 0:HALF]

        def halves(ap):
            return ap.rearrange("p (h c) -> p h c", h=2)

        w_view = {n: w.rearrange("(k p) c -> p k c", p=128)
                  for n, w in (("in", w_in), ("out", w_out), ("up", w_up), ("down", w_down))}
        w_f = w_in.rearrange("(k p) c -> p k c", p=128)[:, :, F_COL:F_COL + NH]
        raw_f = RAW[1][:, :, :].rearrange("p k c -> p (k c)").rearrange("p (k c) -> p k c", k=KT)
        wh_f = WH[1][:, :, :].rearrange("p k c -> p (k c)").rearrange("p (k c) -> p k c", k=KT)
        wl_f = WL[1][:, :, :].rearrange("p k c -> p (k c)").rearrange("p (k c) -> p k c", k=KT)

        def load(sp, u, s, src):
            sp.wait_ge(lo_done, u)
            sp.dma_start(RAW[s][:, :, :], src).then_inc(raw_in[s], 16)

        def load_group(sp, G, srcs):
            for s in range(2):
                load(sp, G * 2 + (s + 1), s, srcs[s])

        def hi(act, G, s):
            act.wait_ge(raw_in[s], G * 16 + 16 * (s + 1))
            act.wait_ge(unit_done, G * 2 + (s + 1))
            act.activation(WH[s][:, :, :], RAW[s][:, :, :], ACT.Copy).then_inc(hi_done, 1)

        def lo(dve, G, s):
            dve.wait_ge(hi_done, G * 2 + (s + 2))
            dve.tensor_tensor(WL[s][:, :, :], RAW[s][:, :, :], WH[s][:, :, :].bitcast(F32),
                              ALU.subtract).then_inc(lo_done, 1)

        def products(pe, m, s, k, kk, X, Y, first, final):
            a, b = WH[s][:, k, 128 * m:128 * m + 128], WL[s][:, k, 128 * m:128 * m + 128]
            last_mm = None
            for n, (w, x) in enumerate(((a, X), (a, Y), (b, X))):
                for h in range(2):
                    last_mm = pe.matmul(PS[:, 2 * m + h, 0:HALF], w, x[:, kk, HALF * h:HALF * h + HALF],
                                        start=(first and n == 0), stop=(final and n == 2))
            return last_mm

        def group(pe, G, Mc, X, Y, ready=None, after_a=None):
            for s in range(2):
                pe.wait_ge(lo_done, G * 2 + (s + 3))
                for m in range(2):
                    if s == 0:
                        pe.wait_ge(ev[m], Mc + 1)
                    for k in range(UK):
                        kk = UK * s + k
                        if ready is not None and m == 0:
                            pe.wait_ge(ready, kk + 1)
                        mm = products(pe, m, s, k, kk, X, Y, kk == 0, kk == KT - 1)
                    if m == 1:
                        mm.then_inc(unit_done, 1)
                    elif s == 1:
                        mm.then_inc(m0_done, 1)
                if s == 0 and after_a is not None:
                    after_a()

        block = ctx.enter_context(nc.Block())

        @block.sync
        def _(sp):
            for t in range(4):
                sp.dma_start(XROW[:, t, :], x_prompt[128 * t:128 * t + 128, :]).then_inc(x_in, 16)
            sp.dma_start(XROWS[:, :], x_sample).then_inc(x_in, 16)
            sp.wait_ge(cf_clear, 1)
            with nc.allow_non_contiguous_dma(reason="4 columns"):
                sp.dma_start(raw_f[:, :, 0:NH], w_f).then_inc(raw_in[1], 16)
            with sp.Fori(0, 20) as i:
                load_group(sp, i, [w_view["in"][:, UK * s:UK * s + UK, bass.ds(i * UC, UC)] for s in range(2)])
            load_group(sp, G_O, [w_view["out"][:, UK * s:UK * s + UK, 0:UC] for s in range(2)])
            for m in range(2):
                sp.wait_ge(stg_out[m], 16 * 13)
            sp.wait_ge(ss_done, NA)
            sp.wait_ge(last_a, 2 * (CONV - 1))

            def load_heads(q, it, kv, kc, vc):
                for par in range(2):
                    hc = it * 2 + (4 * q + par)
                    h = it * 2 + par
                    sp.wait_ge(pv_done, hc + 1)
                    for dst, n in ((QF, 0), (KF, 1), (VF, 2)):
                        sp.dma_start(dst[par][:, :], one_dram(QS, h + NH * (3 * q + n))).then_inc(att_in[par], 16)
                    for dst, src in ((KC, kc), (VC, vc)):
                        sp.dma_start(dst[par][:, :, :], cache_head(src, h)).then_inc(att_in[par], 16)

            with sp.Fori(0, 2) as it:
                load_heads(0, it, None, band_k, band_v)
            with sp.Fori(0, 2) as it:
                load_heads(1, it, None, fox_k, fox_v)
            with sp.Fori(1, 8) as i:
                load_group(sp, i + G_O, [w_view["out"][:, UK * s:UK * s + UK, bass.ds(i * UC, UC)] for s in range(2)])
            with sp.Fori(0, N_CHUNK) as c:
                with sp.Fori(0, 4) as j:
                    load_group(sp, c * 8 + j + G_F,
                               [w_view["up"][:, UK * s:UK * s + UK, bass.ds(c * 1024 + j * UC, UC)] for s in range(2)])
                with sp.Fori(0, 4) as j:
                    load_group(sp, c * 8 + j + (G_F + 4),
                               [w_view["down"][:, bass.ds(c * UK, UK), bass.ds(j * 2 * UC + UC * s, UC)] for s in range(2)])
            for t in range(5):
                sp.wait_ge(out_c, 4 * t + 4)
                if t < 4:
                    sp.dma_start(y_prompt[128 * t:128 * t + 128, :], OUT[t % 2][:, :]).then_inc(out_rows[t % 2], 16)
                else:
                    sp.dma_start(y_sample, OUT[0][0:DEC, :]).then_inc(out_rows[0], 16)
            sp.wait_ge(out_rows[0], 48)
            sp.wait_ge(out_rows[1], 32)
            sp.wait_ge(stores, 16 * 6)
            for p in range(2):
                sp.wait_ge(kv_out[p], 64 * 5)

        @block.scalar
        def _(act):
            chain = Chain(act, act_c)
            rows = [(VR1, 0, g_mix), (VR1, 16, ln1_g), (VR1, 32, ln1_b), (VR1, 48, ln2_g), (VR1, 64, ln2_b),
                    (VR1, 80, w_conv), (VR1, 112, b_conv), (VR1, 120, b_ra),
                    (VR2, 0, b_rx), (VR2, 8, lam), (VR2, 16, state_lru), (VR2, 24, state_conv)]
            for dst, at, src in rows:
                v = src.rearrange("a (t p) -> (a t) p", p=128)
                act.dma_start(dst[at:at + v.shape[0], :], v).then_inc(vec_in, 16)
            act.dma_start(CFL[:, :, :], fox_logf.rearrange("(j p) h -> p j h", p=128)).then_inc(vec_in, 16)
            with nc.allow_non_contiguous_dma(reason="4 numbers"):
                act.dma_start(tiny[0:NH, 0:1], b_forget.rearrange("a h -> h a")).then_inc(vec_in, 16)
            for k in range(KT):
                act.wait_ge(xt_done, k + 1)
                act.activation(XH[:, k, :], PSF[:, 1024 * (k % 4):1024 * (k % 4) + TOK], ACT.Copy).then_inc(xh_done, 1)
            act.wait_ge(raw_in[1], 16)
            act.activation(WH[1][:, :, :], RAW[1][:, :, :], ACT.Copy).then_inc(hi_done, 1)
            act.wait_ge(vec_t, 1)
            act.activation(VT1[:, :], PS[:, 4, 0:128], ACT.Copy).then_inc(vec_done, 1)
            act.activation(VT2[:, :], PS[:, 5, 0:48], ACT.Copy).then_inc(vec_done, 1)
            act.activation(CL[:, :], PS[0:NH, 6, :], ACT.Copy).then_inc(vec_done, 1)
            hi(act, 0, 0)
            act.wait_ge(unit_done, 2)
            act.activation(halves(ZT[:, :]), pair(1, NH), ACT.Identity, bias=tiny[0:NH, 0:1]).then_inc(ev[1], 1)
            hi(act, 0, 1)
            act.wait_ge(vec_done, 3)
            act.wait_ge(ev[1], 1)
            chain(act.activation(ZA[:, :], ZT[:, :], ACT.Abs))
            chain(act.activation(LZ[:, 0, :], VT2[:, 8:16], ACT.Abs))
            chain(act.activation(ZA[:, :], ZA[:, :], ACT.Exp, scale=-1.0))
            act.activation(LZ[:, 0, :], LZ[:, 0, :], ACT.Exp, scale=-1.0).then_inc(z_exp, 1)
            act.wait_ge(z_u, 2)
            act.activation(ZC[:, :], ZB[:, :], ACT.Ln).then_inc(z_ln, 1)
            act.activation(LZ[:, 2, :], LZ[:, 1, :], ACT.Ln).then_inc(z_ln, 1)
            act.wait_ge(ext_out, 16)
            act.wait_ge(xl_done, KT)

            def evac_x(m, i):
                act.wait_ge(*done(m, i + G_A, i + G_A))
                t = i * 2 + m
                act.activation(one(XA, t)[:, CONV - 1:CONV - 1 + HALF], PS[:, 2 * m, 0:HALF], ACT.Copy)
                act.activation(one(XA, t)[:, CONV - 1 + HALF:CONV - 1 + SEQ], PS[:, 2 * m + 1, 0:SEQ - HALF], ACT.Copy)
                act.activation(one(XA, t)[:, S_AT + 3:S_AT + 3 + DEC], PS[:, 2 * m + 1, SEQ - HALF:HALF],
                               ACT.Copy).then_inc(ev[m], 1)

            with act.Fori(0, 4) as i:
                hi(act, i + (G_A + 1), 0)
                evac_x(0, i)
                evac_x(1, i)
                hi(act, i + (G_A + 1), 1)
            with act.Fori(0, 4) as i:
                hi(act, i + (G_A + 5), 0)
                for m in range(2):
                    act.wait_ge(*done(m, i + (G_A + 4), i + (G_A + 4)))
                    act.activation(halves(one(YF, i * 2 + m)), pair(m), ACT.Copy).then_inc(ev[m], 1)
                hi(act, i + (G_A + 5), 1)
            act.wait_ge(ft_done, 1)
            chain(act.activation(LFT[:, 0:4, :], PS[:, 7, 0:16].rearrange("p (t h) -> p t h", h=NH), ACT.Copy))
            chain(act.activation(LFT[0:DEC, 4, :], PS[0:DEC, 7, 16:20], ACT.Copy))
            act.activation(FQ[:, 0:4, :], PS[:, 7, 20:36].rearrange("p (t h) -> p t h", h=NH), ACT.Copy).then_inc(ftc_done, 1)
            act.activation(FQ[0:DEC, 4, :], PS[0:DEC, 7, 36:40], ACT.Copy).then_inc(ftc_done, 1)
            act.dma_start(p_fl.rearrange("(t p) h -> p t h", p=128), LFT[:, 0:4, :]).then_inc(stores, 16)
            act.dma_start(s_fl, LFT[0:DEC, 4, :]).then_inc(stores, 16)

            def stage(m, i):
                act.wait_ge(*done(m, i + G_B, i + G_B))
                act.wait_ge(stg_out[m], i * 16 + 16)
                act.activation(halves(STG[:, m, :]), pair(m), ACT.Copy).then_inc(ev[m], 1)
                act.wait_ge(ev[m], i + (G_B + 2))
                act.dma_start(one_dram(QS, i * 2 + m), STG[:, m, :]).then_inc(stg_out[m], 16)

            with act.Fori(0, NA) as i:
                act.dma_start(WRA[:, :], one_dram(w_ra, i)).then_inc(gw_in, 16)
                act.dma_start(WRX[:, :], one_dram(w_rx, i)).then_inc(gw_in, 16)
                hi(act, i + (G_B + 1), 0)
                chain.enter(i, 1, NA)
                act.wait_ge(gate_done, i + 1)
                chain(act.activation(gate2(TR), PS[:, 4:6, 0:CW // 2], ACT.Tanh, bias=half_b[:, 0, bass.ds(i, 1)], scale=0.5))
                act.activation(AA[:, :], TR[:, :], ACT.Exp, bias=c_sp[:, 0, bass.ds(i, 1)],
                               scale=c_sp[:, 0, bass.ds(i, 1)]).then_inc(a_done, 1)
                act.activation(T1[:, :], TR[:, :], ACT.Tanh, bias=c_sp[:, 1, bass.ds(i, 1)],
                               scale=c_sp[:, 1, bass.ds(i, 1)]).then_inc(a_done, 1)
                act.activation(gate2(TI), PS[:, 6:8, 0:CW // 2], ACT.Tanh, bias=half_b[:, 1, bass.ds(i, 1)],
                               scale=0.5).then_inc(ti_done, 1)
                act.wait_ge(gi_done, i + 1)
                act.activation(TH[:, :], GI[:, :], ACT.Tanh).then_inc(th_done, 1)
                stage(0, i)
                act.wait_ge(m2_done, i + 1)
                act.activation(T1[:, :], T1[:, :], ACT.Sqrt, scale=0.25).then_inc(sq_done, 1)
                stage(1, i)
                hi(act, i + (G_B + 1), 1)
                chain.leave()
            with act.Fori(NA, 12) as i:
                hi(act, i + (G_B + 1), 0)
                stage(0, i)
                stage(1, i)
                hi(act, i + (G_B + 1), 1)

            act.wait_ge(unit_done, 2 * G_O + 2)
            act.activation(R[:, :, :], XL[:, :, :].bitcast(F32), ACT.Copy, scale=ALPHA).then_inc(r_alpha, 1)
            act.wait_ge(ssa_mm, 1)
            act.activation(halves(SSA[:, :]), pair(0), ACT.Sqrt, bias=eps[:, :], scale=1.0 / DA).then_inc(ssa_sd, 1)
            act.wait_ge(r_init, 1)
            for h in range(NH):
                act.wait_ge(fb_mm, 2 * h + 1)
                act.activation(FB[:, h, :], PS[:, 2, :], ACT.Copy).then_inc(fb_done, 1)
                act.wait_ge(fb_mm, 2 * h + 2)
                act.activation(FSB[:, h, :], PSF[:, 2048:2048 + TOK], ACT.Copy).then_inc(fb_done, 1)

            def head(q, it, par, out_k, out_v, new_k, new_v):
                hc = it * 2 + (4 * q + par)
                h = it * 2 + par
                act.wait_ge(tp, hc * 4 + 1)
                act.activation(KCT[:, :], PS[:, 6, :], ACT.Copy).then_inc(tc, 1)
                act.wait_ge(tp, hc * 4 + 2)
                act.wait_ge(kv_out[par], it * 64 + (128 * q + 64))
                act.activation(VT[par][:, 0:4, :], PS[:, 7, :].rearrange("p (j d) -> p j d", d=HD), ACT.Copy).then_inc(tc, 1)
                act.wait_ge(tp, hc * 4 + 3)
                act.activation(KTM[par][:, 0:4, :], PS[:, 6, :].rearrange("p (j d) -> p j d", d=HD), ACT.Copy).then_inc(tc, 1)
                act.wait_ge(tp, hc * 4 + 4)
                act.activation(VT[par][0:DEC, 4, :], PS[0:DEC, 7, 0:HD], ACT.Copy)
                act.activation(KTM[par][0:DEC, 4, :], PS[0:DEC, 7, HD:2 * HD], ACT.Copy).then_inc(tc, 1)
                act.wait_ge(tc, hc * 4 + 4)
                for dst, src in ((cache_head(out_k, h), KTM[par][:, 0:4, :]), (cache_head(out_v, h), VT[par][:, 0:4, :]),
                                 (row_head(new_k, h), KTM[par][0:DEC, 4, :]), (row_head(new_v, h), VT[par][0:DEC, 4, :])):
                    act.dma_start(dst, src).then_inc(kv_out[par], 16)

                def exp(i):
                    n = DEC if i == 4 else 128
                    act.wait_ge(mx, hc * 5 + (i + 1))
                    act.activation(tile_s(i, n), tile_s(i, n), ACT.Exp, bias=small[0:n, i, 0:1],
                                   accum_out=small[0:n, i, 1:2]).then_inc(ex, 1)

                def copy_pt(i):
                    act.wait_ge(pt, hc * 5 + (i + 1))
                    b = 6 + i % 2
                    if i < 4:
                        act.activation(PT[:, 0:i + 1, 128 * i:128 * i + 128],
                                       PS[:, b, 0:128 * (i + 1)].rearrange("p (j c) -> p j c", c=128), ACT.Copy).then_inc(ptc, 1)
                    else:
                        act.activation(PTS[:, 0:4, :], PS[:, b, 0:4 * DEC].rearrange("p (j c) -> p j c", c=DEC), ACT.Copy)
                        act.activation(PTS[0:DEC, 4, :], PS[0:DEC, b, 4 * DEC:5 * DEC], ACT.Copy).then_inc(ptc, 1)

                exp(0)
                for i in range(1, 5):
                    exp(i)
                    copy_pt(i - 1)
                copy_pt(4)
                act.wait_ge(pv_done, hc + 3)
                act.activation(one(YF, h + (NA + NH * q)), PSF[:, 2048:2048 + TOK], ACT.Copy).then_inc(yv, 1)

            with act.Fori(0, 2) as it:
                for par in range(2):
                    head(0, it, par, p_bk, p_bv, s_bk, s_bv)
            act.wait_ge(ya_done, NA)
            with act.Fori(0, 2) as it:
                for par in range(2):
                    head(1, it, par, p_fk, p_fv, s_fk, s_fv)

            act.wait_ge(yv, 9)
            act.wait_ge(mx, 40)
            for t in range(8):
                if t >= 2:
                    act.wait_ge(yss, t - 1)
                act.activation((N2, N3)[t % 2][:, :], YF[:, NA + t, :], ACT.Square).then_inc(ysq, 1)
            for q, n in enumerate((N0, N1)):
                act.wait_ge(y_mm, q + 1)
                act.activation(halves(n[:, :]), pair(q), ACT.Sqrt, bias=eps[:, :], scale=1.0 / (NH * HD)).then_inc(y_sd, 1)
            act.wait_ge(ya_done, NA)
            for k in range(KT):
                if k >= NA:
                    act.wait_ge(y_g, k - NA + 1)
                act.activation(YH[:, k, :], YF[:, k, :], ACT.Copy).then_inc(yh_done, 1)

            act.wait_ge(last_t, 1)
            act.activation(LROW[:, :], PS[0:64, 6, 0:128], ACT.Copy).then_inc(last_c, 1)
            act.wait_ge(last_c, 1)
            for at, dst in ((0, p_conv), (24, s_conv), (48, p_lru), (56, s_lru)):
                v = dst.rearrange("a (t p) -> (a t) p", p=128)
                act.dma_start(v, LROW[at:at + v.shape[0], :]).then_inc(stores, 16)

            with act.Fori(0, 8) as i:
                for s in range(2):
                    hi(act, i + (G_O + 1), s)

            def norm(n, T, shift):
                act.wait_ge(n.mm1, 1)
                act.activation(halves(N1[:, :]), PS[:, 4:6, 0:HALF], ACT.Copy, scale=1.0 / D).then_inc(n.mean, 1)
                with act.Fori(0, KT // 2) as i:
                    for e in range(2):
                        k = i * 2 + e
                        act.wait_ge(n.xc, k + 1)
                        act.wait_ge(n.s2, k + 1)
                        act.activation((N2, N3)[e][:, :], one(T, k), ACT.Square).then_inc(n.sq, 1)
                act.wait_ge(n.mm2, 1)
                act.wait_ge(n.s2, KT + 2)
                act.activation(halves(N2[:, :]), PS[:, 6:8, 0:HALF], ACT.Sqrt, bias=eps[:, :], scale=1.0 / D).then_inc(n.sd, 1)
                with act.Fori(0, KT) as k:
                    act.wait_ge(n.g, k + 1)
                    act.activation(one(T, k), one(T, k), ACT.Identity, bias=shift[:, bass.ds(k, 1)]).then_inc(n.b, 1)
                    if T is R:
                        act.wait_ge(n.b, k + 1)
                        act.activation(one(X1H, k), one(T, k), ACT.Copy).then_inc(x1h_done, 1)

            norm(n1, R, L1B)

            def up(c, j, G, Mc):
                hi(act, G + 1, 0)
                for m in range(2):
                    t = j * 2 + m
                    n = c * 8 + t
                    act.wait_ge(*done(m, G, Mc))
                    act.wait_ge(h_ready, n + 1)
                    act.activation(halves(RT[m][:, :]), pair(m), ACT.Relu).then_inc(ev[m], 1)
                    act.wait_ge(ev[m], Mc + 2)
                    chain(act.activation(RT[m][:, :], RT[m][:, :], ACT.Square))
                    act.activation(one(HHI, t), RT[m][:, :], ACT.Copy).then_inc(hh_done, 1)
                hi(act, G + 1, 1)

            def chunk(c, final):
                with act.Fori(0, 4) as j:
                    chain.enter(j, 2, 4)
                    up(c, j, c * 8 + j + G_F, c * 12 + j + G_F)
                    chain.leave()
                with act.Fori(0, 3 if final else 4) as j:
                    for s in range(2):
                        hi(act, c * 8 + j + (G_F + 5), s)

            with act.Fori(0, N_CHUNK - 1) as c:
                chain.enter(c, 8, N_CHUNK - 1)
                chunk(c, False)
                chain.leave()
            chunk(N_CHUNK - 1, True)
            norm(n2, ACC, L2B)
            for t in range(5):
                n = 128 if t < 4 else DEC
                for q in range(4):
                    act.wait_ge(out_t, 4 * t + q + 1)
                    if t >= 2 and q == 0:
                        act.wait_ge(out_rows[t % 2], 16 * (t // 2))
                    act.activation(OUT[t % 2][0:n, 512 * q:512 * q + 512], PS[0:n, (4 * t + q) % 8, :], ACT.Copy)\
                       .then_inc(out_c, 1)

        @block.vector
        def _(dve):
            chain = Chain(dve, dve_c)
            for s, n in ((lo_done, 1), (unit_done, 1), (ev[0], 1), (stg_out[0], 16), (stg_out[1], 16), (kv_out[0], 64),
                         (kv_out[1], 64), (pv_done, 2), (yv, 1), (n1.s2, 2), (n2.s2, 2), (h_ready, 2)):
                dve.sem_inc(s, n)
            chain(dve.memset(eps[:, :], EPS))
            dve.wait_ge(rel_in, 16)
            chain(dve.tensor_copy(EXT[:, 0:REV], REL[:, NREL - 1:NREL].to_broadcast([NH, REV])))
            dve.tensor_copy(EXT[:, REV:EW], REL[:, NREL - (EW - REV):NREL][:, ::-1]).then_inc(ext_done, 1)
            for k in range(KT):
                dve.wait_ge(xh_done, k + 1)
                dve.tensor_tensor(XL[:, k, :], PSF[:, 1024 * (k % 4):1024 * (k % 4) + TOK], XH[:, k, :].bitcast(F32),
                                  ALU.subtract).then_inc(xl_done, 1)
            dve.wait_ge(hi_done, 1)
            dve.tensor_tensor(WL[1][:, :, :], RAW[1][:, :, :], WH[1][:, :, :].bitcast(F32), ALU.subtract).then_inc(lo_done, 1)
            lo(dve, 0, 0)
            dve.wait_ge(vec_done, 2)
            chain(dve.tensor_scalar(half_b[:, 0, :], VT1[:, 120:128], 0.5, None, ALU.mult))
            chain(dve.tensor_scalar(half_b[:, 1, :], VT2[:, 0:8], 0.5, None, ALU.mult))
            lo(dve, 0, 1)
            dve.wait_ge(z_exp, 1)
            cases = ((ZT[:, :], ZA[:, :], ZB[:, :], ZC[:, :], ZT[:, :]),
                     (VT2[:, 8:16], LZ[:, 0, :], LZ[:, 1, :], LZ[:, 2, :], LZ[:, 3, :]))
            for z, e, u, ln, out in cases:
                dve.tensor_scalar(u, e, 1.0, None, ALU.add).then_inc(z_u, 1)
            dve.wait_ge(z_ln, 2)
            for z, e, u, ln, out in cases:
                chain(dve.tensor_scalar(u, u, 1.0, None, ALU.subtract))
                chain(dve.scalar_tensor_tensor(ln, u, 0.0, ln, ALU.is_equal, ALU.add))
                chain(dve.scalar_tensor_tensor(u, u, 0.0, u, ALU.is_equal, ALU.add))
                chain(dve.reciprocal(u, u))
                chain(dve.tensor_tensor(u, u, e, ALU.mult))
                chain(dve.tensor_tensor(ln, ln, u, ALU.mult))
                chain(dve.scalar_tensor_tensor(out, z, 0.0, ln, ALU.min, ALU.subtract))
            chain(dve.tensor_scalar(c_sp[:, 0, :], LZ[:, 3, :], 4.0, None, ALU.mult))
            chain(dve.tensor_scalar(c_sp[:, 1, :], LZ[:, 3, :], -4.0, None, ALU.mult))
            dve.wait_ge(vec_done, 3)
            chain(dve.memset(ZB[:, :], 1.0))
            chain(dve.tensor_tensor_scan(FP[:, 0:SEQ], ZB[:, 0:SEQ], ZT[:, 0:SEQ], 0.0, ALU.mult, ALU.add))
            chain(dve.tensor_tensor_scan(FS[:, 0:PAST], ZB[:, 0:PAST], CL[:, :], 0.0, ALU.mult, ALU.add))
            dve.tensor_tensor_scan(FS[:, PAST:], ZB[:, 0:DEC], ZT[:, SEQ:], FS[:, PAST - 1:PAST], ALU.mult, ALU.add)\
               .then_inc(f_done, 1)
            with dve.Fori(0, 8) as i:
                for s in range(2):
                    lo(dve, i + (G_A + 1), s)
            dve.wait_ge(xa_init, CONV - 1)
            dve.wait_ge(ev[0], 9)
            dve.wait_ge(ev[1], 9)
            dve.wait_ge(ft_done, 1)
            with dve.Fori(0, NA) as i:
                chain.enter(i, 6, NA)
                xa, g = one(XA, i), one(YF, i)

                def tap(j):
                    return WC[:, bass.ds(i + 8 * j, 1)]

                chain(dve.tensor_scalar(XC[:, :], xa[:, 0:CW], tap(0), BC[:, bass.ds(i, 1)], ALU.mult, ALU.add))
                for j in range(1, CONV - 1):
                    chain(dve.scalar_tensor_tensor(XC[:, :], xa[:, j:j + CW], tap(j), XC[:, :], ALU.mult, ALU.add))
                j = CONV - 1
                dve.scalar_tensor_tensor(XC[:, :], xa[:, j:j + CW], tap(j), XC[:, :], ALU.mult, ALU.add).then_inc(conv_done, 1)
                lo(dve, i + (G_B + 1), 0)
                dve.wait_ge(ti_done, i + 1)
                chain(dve.scalar_tensor_tensor(UX[:, :], TI[:, :], 1.0, XC[:, :], ALU.add, ALU.mult))
                dve.wait_ge(a2_done, i + 1)
                dve.scalar_tensor_tensor(T1[:, :], HS[:, :], 1.0, T1[:, :], ALU.add, ALU.mult).then_inc(m2_done, 1)
                dve.wait_ge(th_done, i + 1)
                dve.scalar_tensor_tensor(GG[:, :], TH[:, :], 1.0, g, ALU.add, ALU.mult)
                dve.wait_ge(sq_fix, i + 1)
                chain(dve.tensor_tensor(UX[:, :], UX[:, :], T1[:, :], ALU.mult))
                dve.tensor_tensor_scan(HS[:, 0:SEQ], AA[:, 0:SEQ], UX[:, 0:SEQ], 0.0, ALU.mult, ALU.add)
                chain(dve.tensor_tensor_scan(HS[:, SEQ:TOK], AA[:, S_AT:S_AT + DEC], UX[:, S_AT:S_AT + DEC],
                                             H0[:, bass.ds(i, 1)], ALU.mult, ALU.add))
                dve.scalar_tensor_tensor(g, HS[:, 0:TOK], 0.5, GG[:, :], ALU.mult, ALU.mult).then_inc(y_done, 1)
                lo(dve, i + (G_B + 1), 1)
                chain.leave()
            with dve.Fori(NA, 12) as i:
                for s in range(2):
                    lo(dve, i + (G_B + 1), s)
            dve.wait_ge(r_alpha, 1)
            dve.scalar_tensor_tensor(flat(R), flat(XH).bitcast(F32), ALPHA, flat(R), ALU.mult, ALU.add).then_inc(r_init, 1)
            dve.wait_ge(ssa_sd, 1)
            dve.reciprocal(SSA[:, :], SSA[:, :]).then_inc(ssa_rs, 1)
            dve.wait_ge(m_done, 1)

            def head(q, it, par):
                hc = it * 2 + (4 * q + par)
                h = it * 2 + par
                chain.enter(it, 20, 2) if par == 0 else None

                def score(i):
                    n = DEC if i == 4 else 128
                    dve.wait_ge(sc, hc * 5 + (i + 1))
                    if q:
                        dve.wait_ge(bf_done, it * 10 + (5 * par + i + 1))
                        bias = BF[0:n, S_OFF[i]:S_OFF[i] + S_LEN[i]]
                    else:
                        at = 0 if i == 4 else 512 - 128 * i
                        bias = one(M, h)[0:n, at:at + S_LEN[i]]
                    src = PSF[0:n, 2048:2048 + TOK] if i == 4 else PS[:, i, 0:S_LEN[i]]
                    chain(dve.scalar_tensor_tensor(tile_s(i, n), src, SCALE, bias, ALU.mult, ALU.add))
                    dve.tensor_reduce(small[0:n, i, 0:1], tile_s(i, n), AX.X, ALU.max, negate=True).then_inc(mx, 1)

                def normalise(i):
                    n = DEC if i == 4 else 128
                    dve.wait_ge(ex, hc * 5 + (i + 1))
                    chain(dve.reciprocal(small[0:n, i, 2:3], small[0:n, i, 1:2]))
                    dve.tensor_scalar(tile_s(i, n), tile_s(i, n), small[0:n, i, 2:3], None, ALU.mult).then_inc(pn, 1)

                score(0)
                for i in range(1, 5):
                    score(i)
                    normalise(i - 1)
                normalise(4)
                if par == 1:
                    chain.leave()

            for q in range(2):
                with dve.Fori(0, 2) as it:
                    for par in range(2):
                        head(q, it, par)
            for q, n in enumerate((N0, N1)):
                dve.wait_ge(y_sd, q + 1)
                chain(dve.reciprocal(n[:, :], n[:, :]))
                for t in range(NH):
                    k = NA + NH * q + t
                    dve.scalar_tensor_tensor(YF[:, k, :], YF[:, k, :], GM[:, k:k + 1], n[:, :], ALU.mult, ALU.mult).then_inc(y_g, 1)
            for p in range(2):
                dve.wait_ge(kv_out[p], 64 * 5)
            for k in range(KT):
                dve.wait_ge(yh_done, k + 1)
                dve.tensor_tensor(YL[:, k, :], YF[:, k, :], YH[:, k, :].bitcast(F32), ALU.subtract).then_inc(y_ready, 1)

            with dve.Fori(0, 8) as i:
                lo(dve, i + (G_O + 1), 0)
                for m in range(2):
                    dve.wait_ge(*done(m, i + G_O, i + G_O))
                    t = halves(one(R, i * 2 + m))
                    ins = dve.tensor_tensor(t, pair(m), t, ALU.add)
                    ins.then_inc(ev[m], 1)
                lo(dve, i + (G_O + 1), 1)

            def norm(n, T, gain):
                dve.wait_ge(ev[0], G_F + 1 + (0 if T is R else 12 * N_CHUNK))
                dve.wait_ge(ev[1], G_F + 1 + (0 if T is R else 12 * N_CHUNK))
                dve.tensor_reduce(N0[:, :], T[:, :, :].rearrange("p k t -> p t k"), AX.X, ALU.add).then_inc(n.s1, 1)
                dve.wait_ge(n.mean, 1)
                with dve.Fori(0, KT) as k:
                    dve.tensor_tensor(one(T, k), one(T, k), N1[:, :], ALU.subtract).then_inc(n.xc, 1)
                dve.wait_ge(n.sd, 1)
                dve.wait_ge(n.xc, KT)
                chain(dve.reciprocal(N1[:, :], N2[:, :]))
                with dve.Fori(0, KT) as k:
                    dve.scalar_tensor_tensor(one(T, k), one(T, k), gain[:, bass.ds(k, 1)], N1[:, :], ALU.mult, ALU.mult)\
                       .then_inc(n.g, 1)

            norm(n1, R, L1G)
            with dve.Fori(0, KT) as k:
                dve.wait_ge(x1h_done, k + 1)
                dve.wait_ge(acc_init, k + 1)
                dve.tensor_tensor(one(X1L, k), one(R, k), one(X1H, k).bitcast(F32), ALU.subtract).then_inc(x1_ready, 1)

            def chunk(c, final):
                with dve.Fori(0, 4) as j:
                    G = c * 8 + j + G_F
                    lo(dve, G + 1, 0)
                    for m in range(2):
                        t = j * 2 + m
                        dve.wait_ge(hh_done, c * 8 + t + 1)
                        dve.tensor_tensor(one(HLO, t), RT[m][:, :], one(HHI, t).bitcast(F32), ALU.subtract).then_inc(h_ready, 1)
                    lo(dve, G + 1, 1)

                def down(j, prefetch):
                    G = c * 8 + j + (G_F + 4)
                    for s in range(2):
                        for m in range(2):
                            dve.wait_ge(*done_down(m, s, c, j))
                            t = halves(one(ACC, j * 4 + (2 * s + m)))
                            dve.tensor_tensor(t, pair(m), t, ALU.add).then_inc(ev[m], 1)
                        if prefetch:
                            lo(dve, G + 1, s)

                with dve.Fori(0, 3 if final else 4) as j:
                    down(j, True)
                if final:
                    down(3, False)

            with dve.Fori(0, N_CHUNK - 1) as c:
                chunk(c, False)
            chunk(N_CHUNK - 1, True)
            norm(n2, ACC, L2G)

        @block.gpsimd
        def _(pool):
            chain = Chain(pool, pool_c)
            pool.memset(raw_f, 0.0).then_inc(cf_clear, 1)
            chain(pool.memset(ident[:, :], 0.0))
            pool.affine_select(out=ident[:, :], in_=ident[:, :], compare_op=ALU.not_equal, fill=1.0, base=0,
                               pattern=[[-1, 128]], channel_multiplier=1).then_inc(const_done, 1)
            pool.memset(ones[:, :], 1.0).then_inc(const_done, 1)
            chain(pool.memset(sel[:, :, :], 0.0))
            pool.affine_select(out=sel[:, :, :], in_=sel[:, :, :], compare_op=ALU.not_equal, fill=1.0, base=0,
                               pattern=[[-1, NH], [0, 128]], channel_multiplier=1).then_inc(const_done, 1)
            pool.dma_start(REL[:, :], rel_bias).then_inc(rel_in, 16)
            pool.wait_ge(ext_done, 1)
            pool.dma_start(EXD, EXT[:, :]).then_inc(ext_out, 16)
            pool.wait_ge(ext_out, 16)
            for h in range(NH):
                pool.dma_start(REP[h], bass.AP(tensor=EXD.tensor, offset=EW * h, ap=[[0, 128], [1, EW]])).then_inc(rep_out, 16)
            pool.wait_ge(rep_out, 16 * NH)
            for h in range(NH):
                pool.dma_start(M[:, h, :], bass.AP(tensor=REP.tensor, offset=128 * EW * h + 127, ap=[[EW - 1, 128], [1, BW]]))\
                    .then_inc(m_in, 16)
            pool.wait_ge(xl_done, KT)
            pool.wait_ge(vec_done, 2)
            chain(pool.memset(XA[:, :, 0:CONV - 1], 0.0))
            chain(pool.memset(XA[:, :, XW - 2:XW], 0.0))
            chain(pool.memset(SSA[:, :], 0.0))
            for j in range(CONV - 1):
                pool.tensor_copy(XA[:, :, S_AT + j], SC[:, 8 * j:8 * j + 8]).then_inc(xa_init, 1)
            pool.wait_ge(m_in, 16 * NH)
            pool.memset(M[0:64, :, BW - 64:BW], NEG).then_inc(m_done, 1)
            pool.wait_ge(ev[0], 5)
            pool.wait_ge(ev[1], 5)
            for j in range(CONV - 1):
                pool.tensor_copy(last[:, 8 * j:8 * j + 8], XA[:, :, SEQ + j]).then_inc(last_a, 1)
                pool.tensor_copy(last[:, 24 + 8 * j:32 + 8 * j], XA[:, :, S_AT + DEC + j]).then_inc(last_a, 1)
            pool.wait_ge(ev[0], 9)
            pool.wait_ge(ev[1], 9)
            with pool.Fori(0, NA) as i:
                chain.enter(i, 5, NA)
                g = one(YF, i)
                chain(pool.tensor_tensor(GI[:, :], g, g, ALU.mult))
                settle(pool)
                chain(pool.tensor_scalar(GI[:, :], GI[:, :], GELU1, GELU0, ALU.mult, ALU.add))
                settle(pool)
                pool.tensor_tensor(GI[:, :], GI[:, :], g, ALU.mult).then_inc(gi_done, 1)
                pool.wait_ge(a_done, i * 2 + 2)
                settle(pool)
                pool.tensor_tensor(HS[:, :], AA[:, :], AA[:, :], ALU.mult).then_inc(a2_done, 1)
                pool.wait_ge(sq_done, i + 1)
                settle(pool)
                pool.memset(T1[:, 0:1], 0.5).then_inc(sq_fix, 1)
                pool.wait_ge(y_done, i + 1)
                settle(pool)
                chain(pool.tensor_copy(last[:, bass.ds(i + 48, 1)], HS[:, SEQ - 1:SEQ]))
                chain(pool.tensor_copy(last[:, bass.ds(i + 56, 1)], HS[:, TOK - 1:TOK]))
                settle(pool)
                chain(pool.tensor_tensor(GI[:, :], g, g, ALU.mult))
                settle(pool)
                pool.tensor_tensor(SSA[:, :], SSA[:, :], GI[:, :], ALU.add).then_inc(ss_done, 1)
                pool.wait_ge(ss_done, i + 1)
                chain.leave()
            pool.wait_ge(ssa_rs, 1)
            for k in range(NA):
                chain(pool.tensor_scalar(YF[:, k, :], YF[:, k, :], GM[:, k:k + 1], None, ALU.mult))
                pool.tensor_tensor(YF[:, k, :], YF[:, k, :], SSA[:, :], ALU.mult).then_inc(ya_done, 1)
            pool.wait_ge(fb_done, 2 * NH)
            pool.wait_ge(ftc_done, 2)
            for h in range(NH):
                for i in range(5):
                    n = DEC if i == 4 else 128
                    src = FSB[0:n, h, :] if i == 4 else FB[:, h, 0:S_LEN[i]]
                    at = BF[0:n, S_OFF[i]:S_OFF[i] + S_LEN[i]]
                    diag = BF[0:n, S_OFF[i] + S_LEN[i] - n:S_OFF[i] + S_LEN[i]]
                    pool.wait_ge(mx, 5 * (h + NH - 1) + (i + 1 if h else 5))
                    chain(pool.tensor_scalar(at, src, -1.0, FQ[0:n, i, h:h + 1], ALU.mult, ALU.add))
                    pool.affine_select(out=diag, in_=diag, compare_op=ALU.is_ge, fill=NEG, base=0,
                                       pattern=[[-1, n]], channel_multiplier=1).then_inc(bf_done, 1)
            for t in range(8):
                n = (N0, N1)[t // 4]
                pool.wait_ge(ysq, t + 1)
                if t % 4 == 0:
                    pool.tensor_copy(n[:, :], (N2, N3)[t % 2][:, :]).then_inc(yss, 1)
                else:
                    pool.tensor_tensor(n[:, :], n[:, :], (N2, N3)[t % 2][:, :], ALU.add).then_inc(yss, 1)
                pool.wait_ge(yss, t + 1)

            def norm(n):
                pool.wait_ge(n.mm1, 1)
                chain(pool.memset(N0[:, :], 0.0))
                with pool.Fori(0, KT // 2) as i:
                    for e in range(2):
                        k = i * 2 + e
                        pool.wait_ge(n.sq, k + 1)
                        pool.tensor_tensor(N0[:, :], N0[:, :], (N2, N3)[e][:, :], ALU.add).then_inc(n.s2, 1)
                        pool.wait_ge(n.s2, k + 3)

            norm(n1)
            pool.wait_ge(y_ready, KT)
            for k in range(KT):
                pool.wait_ge(n1.b, k + 1)
                pool.tensor_scalar(ACC[:, k, :], R[:, k, :], ALPHA, None, ALU.mult).then_inc(acc_init, 1)
            norm(n2)

        @block.tensor
        def _(pe):
            pe.wait_ge(const_done, 3)
            pe.wait_ge(x_in, 80)
            for k in range(KT):
                if k >= 4:
                    pe.wait_ge(xl_done, k - 3)
                b = 2 * (k % 4)
                for t in range(4):
                    pe.transpose(PS[:, b, 128 * t:128 * t + 128], XROW[:, t, 128 * k:128 * k + 128], ident[:, :])
                pe.transpose(PS[:, b + 1, 0:DEC], XROWS[:, 128 * k:128 * k + 128], ident[0:DEC, 0:DEC]).then_inc(xt_done, 1)
            pe.wait_ge(vec_in, 16 * 14)
            pe.wait_ge(xl_done, KT)
            pe.transpose(PS[:, 4, 0:128], VR1[:, :], ident[:, :])
            pe.transpose(PS[:, 5, 0:48], VR2[:, :], ident[0:48, 0:48])
            for j in range(4):
                t = pe.transpose(PS[0:NH, 6, 128 * j:128 * j + 128], CFL[:, j, :], ident[:, :])
            t.then_inc(vec_t, 1)
            pe.wait_ge(lo_done, 2)
            n = 0
            for w, x in ((wh_f, XH), (wh_f, XL), (wl_f, XH)):
                for k in range(KT):
                    for h in range(2):
                        mm = pe.matmul(PS[:, 2 + h, 0:HALF], w[:, k, :], x[:, k, HALF * h:HALF * h + HALF],
                                       start=(n == 0), stop=(n == 3 * KT - 1))
                    n += 1
            mm.then_inc(unit_done, 1)
            with pe.Fori(0, 8) as i:
                group(pe, i + G_A, i + G_A, XH, XL)
            pe.wait_ge(f_done, 1)
            for t in range(4):
                pe.transpose(PS[:, 7, 4 * t:4 * t + 4], ZT[:, 128 * t:128 * t + 128], ident[0:NH, 0:NH])
                pe.transpose(PS[:, 7, 20 + 4 * t:24 + 4 * t], FP[:, 128 * t:128 * t + 128], ident[0:NH, 0:NH])
            pe.transpose(PS[0:DEC, 7, 16:20], ZT[:, SEQ:TOK], ident[0:NH, 0:NH])
            pe.transpose(PS[0:DEC, 7, 36:40], FS[:, PAST:PAST + DEC], ident[0:NH, 0:NH]).then_inc(ft_done, 1)
            pe.wait_ge(ftc_done, 2)
            with pe.Fori(0, NA) as i:
                def gates():
                    pe.wait_ge(gw_in, i * 32 + 32)
                    pe.wait_ge(conv_done, i + 1)
                    for b, w in ((4, WRA), (6, WRX)):
                        for h in range(2):
                            g = pe.matmul(PS[:, b + h, 0:CW // 2], w[:, :], XC[:, CW // 2 * h:CW // 2 * (h + 1)],
                                          start=True, stop=True)
                    g.then_inc(gate_done, 1)

                group(pe, i + G_B, i + G_B, XH, XL, after_a=gates)
            with pe.Fori(NA, 12) as i:
                group(pe, i + G_B, i + G_B, XH, XL)
            pe.wait_ge(ss_done, NA)
            pe.wait_ge(ev[0], G_O + 1)
            for h in range(2):
                mm = pe.matmul(PS[:, h, 0:HALF], ones[:, :], SSA[:, HALF * h:HALF * h + HALF], start=True, stop=True)
            mm.then_inc(ssa_mm, 1)
            pe.wait_ge(ev[1], G_O + 1)
            for h in range(NH):
                if h:
                    pe.wait_ge(fb_done, 2 * h - 1)
                pe.matmul(PS[:, 2, :], sel[:, h, :], FP[:, 0:SEQ], start=True, stop=True).then_inc(fb_mm, 1)
                if h:
                    pe.wait_ge(fb_done, 2 * h)
                pe.matmul(PS[:, 4, :], sel[:, h, :], FS[:, 0:512], start=True, stop=True)
                pe.matmul(PS[:, 5, 0:DEC], sel[:, h, :], FS[:, 512:], start=True, stop=True).then_inc(fb_mm, 1)
            pe.wait_ge(ssa_sd, 1)
            pe.wait_ge(fb_done, 2 * NH)

            def head(q, it, par):
                hc = it * 2 + (4 * q + par)
                pe.wait_ge(att_in[par], it * 80 + (160 * q + 80))
                for j in range(4):
                    t = pe.transpose(PS[:, 6, 128 * j:128 * j + 128], KC[par][:, j, :], ident[:, :])
                t.then_inc(tp, 1)
                for j in range(4):
                    t = pe.transpose(PS[:, 7, 128 * j:128 * j + 128], VF[par][:, 128 * j:128 * j + 128], ident[:, :])
                t.then_inc(tp, 1)
                pe.wait_ge(tc, hc * 4 + 2)
                for j in range(4):
                    t = pe.transpose(PS[:, 6, 128 * j:128 * j + 128], KF[par][:, 128 * j:128 * j + 128], ident[:, :])
                t.then_inc(tp, 1)
                pe.transpose(PS[0:DEC, 7, 0:HD], VF[par][:, SEQ:TOK], ident[:, :])
                pe.transpose(PS[0:DEC, 7, HD:2 * HD], KF[par][:, SEQ:TOK], ident[:, :]).then_inc(tp, 1)
                for i in range(4):
                    pe.matmul(PS[:, i, 0:S_LEN[i]], QF[par][:, 128 * i:128 * i + 128], KF[par][:, 0:S_LEN[i]],
                              start=True, stop=True).then_inc(sc, 1)
                pe.wait_ge(yv, hc + 1)
                pe.matmul(PS[0:DEC, 4, :], QF[par][:, SEQ:TOK], KCT[:, :], start=True, stop=True)
                pe.matmul(PS[0:DEC, 5, 0:DEC], QF[par][:, SEQ:TOK], KF[par][:, SEQ:TOK], start=True, stop=True).then_inc(sc, 1)
                for i in range(5):
                    n = DEC if i == 4 else 128
                    b = 6 + i % 2
                    pe.wait_ge(pn, hc * 5 + (i + 1))
                    if i < 2:
                        pe.wait_ge(tc, hc * 4 + (3 + i))
                    else:
                        pe.wait_ge(ptc, hc * 5 + (i - 1))
                    settle(pe)
                    for j in range(i + 1):
                        w = min(128, S_LEN[i] - 128 * j)
                        t = pe.transpose(PS[0:w, b, n * j:n * j + n], tile_s(i, n)[:, 128 * j:128 * j + w], ident[0:n, 0:n])
                    t.then_inc(pt, 1)
                pe.wait_ge(ptc, hc * 5 + 5)
                for j in range(4):
                    pe.matmul(PS[:, 4, 128 * j:SEQ], VT[par][:, j, :], PT[:, j, 128 * j:SEQ], start=(j == 0), stop=(j == 3))
                for j in range(4):
                    pe.matmul(PS[:, 5, 0:DEC], VC[par][:, j, :], PTS[:, j, :], start=(j == 0), stop=False)
                pe.matmul(PS[:, 5, 0:DEC], VT[par][0:DEC, 4, :], PTS[0:DEC, 4, :], start=False, stop=True).then_inc(pv_done, 1)

            for q in range(2):
                with pe.Fori(0, 2) as it:
                    for par in range(2):
                        head(q, it, par)
            for q, n in enumerate((N0, N1)):
                pe.wait_ge(yss, 4 * q + 4)
                for h in range(2):
                    mm = pe.matmul(PS[:, 2 * q + h, 0:HALF], ones[:, :], n[:, HALF * h:HALF * h + HALF], start=True, stop=True)
                mm.then_inc(y_mm, 1)
            pe.wait_ge(last_a, 2 * (CONV - 1))
            pe.wait_ge(ss_done, NA)
            pe.transpose(PS[0:64, 6, 0:128], last[:, :], ident[:, :]).then_inc(last_t, 1)
            pe.wait_ge(y_sd, 2)
            with pe.Fori(0, 8) as i:
                group(pe, i + G_O, i + G_O, YH, YL, ready=y_ready)

            def norm(n):
                pe.wait_ge(n.s1, 1)
                for h in range(2):
                    mm = pe.matmul(PS[:, 4 + h, 0:HALF], ones[:, :], N0[:, HALF * h:HALF * h + HALF], start=True, stop=True)
                mm.then_inc(n.mm1, 1)
                pe.wait_ge(n.s2, KT + 2)
                for h in range(2):
                    mm = pe.matmul(PS[:, 6 + h, 0:HALF], ones[:, :], N0[:, HALF * h:HALF * h + HALF], start=True, stop=True)
                mm.then_inc(n.mm2, 1)

            norm(n1)
            with pe.Fori(0, N_CHUNK) as c:
                with pe.Fori(0, 4) as j:
                    group(pe, c * 8 + j + G_F, c * 12 + j + G_F, X1H, X1L, ready=x1_ready)
                with pe.Fori(0, 4) as j:
                    for s in range(2):
                        pe.wait_ge(lo_done, c * 16 + j * 2 + (2 * (G_F + 4) + s + 3))
                        for m in range(2):
                            pe.wait_ge(ev[m], c * 12 + j * 2 + (G_F + 4 + s + 1))
                            for k in range(UK):
                                if s == 0 and m == 0:
                                    pe.wait_ge(h_ready, c * 8 + (k + 3))
                                mm = products(pe, m, s, k, k, HHI, HLO, k == 0, k == UK - 1)
                            mm.then_inc(unit_done if m else m0_done, 1)
            norm(n2)
            pe.wait_ge(n2.b, KT)
            for t in range(5):
                n = 128 if t < 4 else DEC
                for q in range(4):
                    if 4 * t + q >= 8:
                        pe.wait_ge(out_c, 4 * t + q - 7)
                    for e in range(4):
                        tt = pe.transpose(PS[0:n, (4 * t + q) % 8, 128 * e:128 * e + 128],
                                          ACC[:, 4 * q + e, 128 * t:128 * t + n], ident[:, :])
                    tt.then_inc(out_t, 1)


_INS = ["x_prompt", "x_sample", "state_conv", "state_lru", "cache_band_k", "cache_band_v", "cache_fox_k", "cache_fox_v",
        "cache_fox_logf", "w_in", "w_conv", "b_conv", "w_rg_a", "b_rg_a", "w_rg_x", "b_rg_x", "lru_lambda", "rel_bias",
        "b_forget", "g_mix", "w_out", "ln1_g", "ln1_b", "w_up", "w_down", "ln2_g", "ln2_b"]
_IN_SHAPES = {
    "x_prompt": (SEQ, D), "x_sample": (DEC, D), "state_conv": (CONV - 1, DA), "state_lru": (1, DA),
    "cache_band_k": (PAST, NH, HD), "cache_band_v": (PAST, NH, HD), "cache_fox_k": (PAST, NH, HD),
    "cache_fox_v": (PAST, NH, HD), "cache_fox_logf": (PAST, NH), "w_in": (D, D_IN), "w_conv": (CONV, DA),
    "b_conv": (1, DA), "w_rg_a": (NA, HD, HD), "b_rg_a": (1, DA), "w_rg_x": (NA, HD, HD), "b_rg_x": (1, DA),
    "lru_lambda": (1, DA), "rel_bias": (NH, NREL), "b_forget": (1, NH), "g_mix": (1, D), "w_out": (D, D),
    "ln1_g": (1, D), "ln1_b": (1, D), "w_up": (D, DFF), "w_down": (DFF, D), "ln2_g": (1, D), "ln2_b": (1, D)}
_OUTS = [((SEQ, D), (1, SEQ, D)), ((DEC, D), (1, DEC, D)),
         ((CONV - 1, DA), (1, 1, CONV - 1, DA)), ((1, DA), (1, 1, DA))] \
    + [((SEQ, NH, HD), (1, 1, SEQ, NH, HD))] * 4 + [((SEQ, NH), (1, 1, SEQ, NH))] \
    + [((CONV - 1, DA), (1, 1, CONV - 1, DA)), ((1, DA), (1, 1, DA))] \
    + [((DEC, NH, HD), (1, 1, DEC, NH, HD))] * 4 + [((DEC, NH), (1, 1, DEC, NH))]


def kernel(**inputs):
    import numpy as _np
    import concourse.bacc as _bacc
    from concourse.bass_utils import run_bass_kernel_spmd as _run

    nc = _bacc.Bacc("TRN2", target_bir_lowering=False, num_devices=1)
    arrays, args = {}, []
    for name in _INS:
        a = _np.ascontiguousarray(inputs[name]).reshape(_IN_SHAPES[name])
        arrays[f"in_{name}"] = a
        args.append(nc.dram_tensor(f"in_{name}", a.shape, F32, kind="ExternalInput").ap())
    for i, (shape, _) in enumerate(_OUTS):
        args.append(nc.dram_tensor(f"out_{i}", shape, F32, kind="ExternalOutput").ap())
    encoder_step(nc, *args)
    r = _run(nc, [arrays], core_ids=[0])
    return tuple(r.results[0][f"out_{i}"].reshape(full) for i, (_, full) in enumerate(_OUTS))
```

```python
import concourse.bass as bass
from concourse import mybir
from contextlib import ExitStack

F32, F32R = mybir.dt.float32, mybir.dt.float32r
ALU, ACT, AX = mybir.AluOpType, mybir.ActivationFunctionType, mybir.AxisListType

D, SEQ, DEC, PAST, HD, DA, DFF = 2048, 512, 64, 512, 128, 1024, 8192
TOK, HALF = SEQ + DEC, (SEQ + DEC) // 2
KT = D // 128
NA = DA // 128
NH = 4
CONV = 4
NREL, CLIP = 513, 256
D_IN = 2 * DA + 6 * NH * HD + NH
F_COL = D_IN - NH
ALPHA, SCALE, EPS, NEG = 2.0 ** 0.25, HD ** -0.5, 1e-5, -1e30
GELU0 = 0.7978845608028654
GELU1 = GELU0 * 0.044715
UK, UC = 8, 256

G_A = 0
G_B = G_A + 8
G_O1 = G_B + 12
G_O2 = G_O1 + 4
G_U0 = G_O2 + 4
G_D0 = G_U0 + 4
G_C = G_D0 + 4
N_CHUNK, FT = 8, 8
MID = N_CHUNK - 2
G_U7 = G_C + 8 * MID
G_D7 = G_U7 + 4
C_O1 = G_O1
C_O2 = C_O1 + 8
C_U0 = C_O2 + 8
C_D0 = C_U0 + 4
C_C = C_D0 + 8
C_U7 = C_C + 12 * MID
C_D7 = C_U7 + 4
SHIFT = (8, -8)
TX = TOK + 2
TT = 5
XW = 584
CW = 580
S_AT = SEQ + CONV - 1
S_LEN = [128, 256, 384, SEQ, PAST + DEC]
S_OFF = [0, 128, 384, 768, 1280]
S_ALL = sum(S_LEN)
BW = 640
REV = BW - 1 - CLIP
EW = 768


def encoder_step(nc, x_prompt, x_sample, state_conv, state_lru, band_k, band_v, fox_k, fox_v, fox_logf,
                 w_in, w_conv, b_conv, w_ra, b_ra, w_rx, b_rx, lam, rel_bias, b_forget, g_mix, w_out,
                 ln1_g, ln1_b, w_up, w_down, ln2_g, ln2_b,
                 y_prompt, y_sample, p_conv, p_lru, p_bk, p_bv, p_fk, p_fv, p_fl,
                 s_conv, s_lru, s_bk, s_bv, s_fk, s_fv, s_fl):
    ctx = ExitStack()
    with ctx:
        def sb(name, shape, dt=F32):
            return ctx.enter_context(nc.sbuf_tensor(name, shape, dt))

        def sem(name):
            return ctx.enter_context(nc.semaphore(name))

        class Region:
            def __init__(self):
                self.stack = ExitStack()

            def sb(self, name, shape, dt=F32):
                return self.stack.enter_context(nc.sbuf_tensor(name, shape, dt))

            def close(self):
                self.stack.close()

        RAW = [sb(f"raw{s}", [128, UK, UC]) for s in range(2)]
        WH = [sb(f"w_hi{s}", [128, UK, UC], F32R) for s in range(2)]
        WL = [sb(f"w_lo{s}", [128, UK, UC], F32R) for s in range(2)]
        ident = sb("ident", [128, 128])
        ones = sb("ones", [128, 128])
        sel = sb("sel", [NH, NH, 128])
        VT1 = sb("vec1", [128, 96])
        VT2 = sb("vec2", [128, 48])
        half_b = sb("half_b", [128, 2, NA])
        c_sp = sb("c_sp", [128, 2, NA])
        last = sb("last", [128, 64])
        LROW = sb("last_rows", [64, 128])
        eps = sb("eps", [128, 1])
        tiny = sb("tiny", [128, 8])
        small = sb("small", [128, 5, 3])
        LFT = sb("logf_rows", [128, 5, NH])
        FQ = sb("f_rows", [128, 5, NH])
        wb = sb("w_up_shift", [128, 2])
        alpha_b = sb("alpha_b", [128, KT])
        MV = sb("row_mean_var", [128, TT, 2])
        RST = sb("row_rstd", [128, TT])
        GM, L1G, L1B = (VT1[:, 16 * i:16 * i + 16] for i in range(3))
        WC, BC = VT1[:, 48:80], VT1[:, 80:88]
        H0, SC = VT2[:, 16:24], VT2[:, 24:48]

        r = Region()
        M = r.sb("band_bias", [128, NH, BW])
        r.close()
        r = Region()
        BF = r.sb("fox_bias", [128, S_ALL])
        r.close()
        r = Region()
        Q0, Q1, Q2, Q3 = (r.sb(f"rms{i}", [128, TOK]) for i in range(4))
        r.close()
        r = Region()
        RT = [r.sb(f"relu{m}", [128, TOK]) for m in range(2)]
        RS = r.sb("rstd", [128, TOK])
        ST = r.sb("row_stats", [128, TT, 8, 6])
        r.close()
        sb("extra", [128, NH * BW])
        r = Region()
        XL = r.sb("x_lo", [128, KT, TX], F32R)
        r.close()
        r = Region()
        X1L = r.sb("x1_lo", [128, KT, TX], F32R)
        r.close()
        r = Region()
        ROW_S = r.sb("y_rows_s", [DEC, D])
        GR, BR = r.sb("ln2_g_rows", [128, D]), r.sb("ln2_b_rows", [128, D])
        r.close()
        R = sb("resid", [128, KT, TX])
        r = Region()
        XH = r.sb("x_hi", [128, KT, TOK], F32R)
        r.close()
        r = Region()
        YH = r.sb("y_hi", [128, KT, TOK], F32R)
        r.close()
        r = Region()
        X1H = r.sb("x1_hi", [128, KT, TX], F32R)
        r.close()
        r = Region()
        ROWS = r.sb("y_rows", [128, 4, D])
        r.close()
        r = Region()
        r.sb("y_hi_a", [128, NA * TOK])
        S = r.sb("scores", [128, S_ALL])
        PT = r.sb("probs_t", [128, 4, SEQ])
        PTS = r.sb("probs_t_s", [128, 5, DEC])
        r.close()
        sb("region_x", [128, KT * TX])
        r = Region()
        XROW = r.sb("x_rows", [128, 4, D])
        VR1 = r.sb("vec_rows1", [96, 128])
        VR2 = r.sb("vec_rows2", [48, 128])
        CFL = r.sb("cache_logf", [128, 4, NH])
        r.close()
        r = Region()
        YF = r.sb("y_f32", [128, KT, TOK])
        r.close()
        r = Region()
        YL = r.sb("y_lo", [128, KT, TOK], F32R)
        r.close()
        r = Region()
        r.sb("gates", [128, NA * TOK])
        STG = r.sb("stage", [128, 2, TOK])
        GI = r.sb("gelu_in", [128, TOK])
        TH = r.sb("gelu_tanh", [128, TOK])
        GG = r.sb("gelu_gg", [128, TOK])
        FP = r.sb("f_cum_prompt", [NH, TOK])
        FS = r.sb("f_cum_sample", [NH, PAST + DEC])
        SSA = r.sb("ss_a", [128, TOK])
        r.close()
        ACC = sb("acc", [128, KT, TOK])
        r = Region()
        XROWS = r.sb("x_rows_s", [DEC, D])
        REL = r.sb("rel_table", [NH, NREL])
        EXT = r.sb("rel_reversed", [NH, EW])
        r.sb("x_lo_gap", [128, NA * XW - D - NREL - EW])
        ZT, ZA, ZB, ZC = (r.sb(n, [NH, TOK]) for n in ("z", "za", "zb", "zc"))
        CL = r.sb("cache_logf_t", [NH, PAST])
        LZ = r.sb("lz", [128, 4, NA])
        r.close()
        r = Region()
        XA = r.sb("conv_in", [128, NA, XW])
        XC, TR, TI, AA, T1, UX, HS = (r.sb(n, [128, CW]) for n in ("xc", "tr", "ti", "a", "t1", "u", "h"))
        WRA, WRX = (r.sb(n, [128, HD]) for n in ("w_ra", "w_rx"))
        r.close()
        r = Region()
        QF, KF, VF = ([r.sb(f"{n}{i}", [128, TOK]) for i in range(2)] for n in "qkv")
        KC = r.sb("kc", [128, 4, HD])
        VC = [r.sb(f"vc{i}", [128, 4, HD]) for i in range(2)]
        FB = r.sb("f_all", [128, SEQ + PAST + DEC])
        KCT = r.sb("kct", [128, PAST])
        VT, KTM = ([r.sb(f"{n}t{i}", [128, 5, HD]) for i in range(2)] for n in "vk")
        r.close()
        r = Region()
        NS, NQ0, NQ1, NQ2, ND = (r.sb(n, [128, TOK]) for n in ("ln1_sum", "ln1_sq0", "ln1_sq1", "ln1_sq2", "ln1_sd"))
        NQ = [NQ0, NQ1, NQ2]
        r.close()
        r = Region()
        HHI = r.sb("h_hi", [128, FT, TOK], F32R)
        HLO = r.sb("h_lo", [128, FT, TOK], F32R)
        r.close()
        sb("region_h", [128, KT * TOK])
        PS = ctx.enter_context(nc.psum_tensor("psum", [128, 8, 512], F32))
        PSF = PS[:, :, :].rearrange("p b c -> p (b c)")
        QS = nc.dram_tensor("qkv_scratch", [6 * NH, 128, TOK], F32).ap()
        EXD = nc.dram_tensor("rel_reversed_dram", [NH, EW], F32).ap()
        FD = nc.dram_tensor("f_dram", [NH, SEQ + PAST + DEC], F32).ap()
        REP = nc.dram_tensor("rel_repeated", [NH, 128, EW], F32).ap()

        raw_in = [sem(f"raw_in{s}") for s in range(2)]
        hi_done, lo_done = sem("hi_done"), sem("lo_done")
        unit_done = sem("unit_done")
        m0_done = sem("m0_done")
        ev = [sem(f"evacuated{m}") for m in range(2)]
        x_in = [sem(f"x_in{p}") for p in range(2)]
        vec_in, cf_clear = sem("vec_in"), sem("cf_clear")
        const_done, vec_t, vec_done = sem("const_done"), sem("vec_t"), sem("vec_done")
        xt_done, xh_done, xl_done = sem("xt_done"), sem("xh_done"), sem("xl_done")
        rel_in, ext_done, ext_out, rep_out = sem("rel_in"), sem("ext_done"), sem("ext_out"), sem("rep_out")
        m_in, m_done, pool_m = sem("m_in"), sem("m_done"), sem("pool_m")
        act_c, dve_c, pool_c = sem("act_chain"), sem("dve_chain"), sem("pool_chain")
        z_abs, z_exp, z_u, z_ln, z_fwd = sem("z_abs"), sem("z_exp"), sem("z_u"), sem("z_ln"), sem("z_fwd")
        f_done, ft_done, ftc_done = sem("f_done"), sem("ft_done"), sem("ftc_done")
        xa_init, last_a = sem("xa_init"), sem("last_a")
        gw_in, conv_done, gate_done = sem("gate_w_in"), sem("conv_done"), sem("gate_done")
        a_done, ti_done, th_done, gi_done = sem("a_done"), sem("ti_done"), sem("th_done"), sem("gi_done")
        a2_done, m2_done, sq_done, sq_fix = sem("a2_done"), sem("m2_done"), sem("sq_done"), sem("sq_fix")
        scan_done, y_done, ss_done = sem("scan_done"), sem("y_done"), sem("ss_done")
        stg_done = sem("stg_done")
        stg_out = [sem(f"stg_out{m}") for m in range(2)]
        r_alpha, r_init = sem("r_alpha"), sem("r_init")
        ssa_mm, ssa_sd, ssa_rs, ya_done = sem("ssa_mm"), sem("ssa_sd"), sem("ssa_rs"), sem("ya_done")
        fd_out, fb_in = sem("fd_out"), sem("fb_in")
        att_in = [sem(f"att_in{i}") for i in range(2)]
        kv_out = [sem(f"kv_out{i}") for i in range(2)]
        tp, tc, sc, mx, ex, pn = (sem(n) for n in ("tp", "tc", "sc", "mx", "ex", "pn"))
        pt, ptc, bf_done = sem("pt"), sem("ptc"), sem("bf_done")
        pv_done, yv = sem("pv_done"), sem("yv")
        ysq, yss, y_mm, y_sd, y_rs, y_g = (sem(n) for n in ("ysq", "yss", "y_mm", "y_sd", "y_rs", "y_g"))
        yh_done, y_ready = sem("yh_done"), sem("y_ready")
        r_done = sem("r_done")
        x1h_done, acc_init, x1_ready = sem("x1h_done"), sem("acc_init"), sem("x1_ready")
        hh_done, h_ready, acc_done = sem("hh_done"), sem("h_ready"), sem("acc_done")
        settled = sem("settled")
        last_t, last_c = sem("last_t"), sem("last_c")
        stores = sem("stores")
        ln_sum, ln_mm1, ln_xc, ln_sq, ln_ss, ln_mm2, ln_sd, ln_rs = (
            sem(f"ln1_{n}") for n in ("sum", "mm1", "centred", "squared", "sumsq", "mm2", "sd", "rstd"))
        b_hi, acc_mul = sem("b_hi"), sem("acc_mul")
        gb_in, rows_t, rows_c = sem("gain_shift_in"), sem("rows_t"), sem("rows_c")
        stats_done, row_sd, row_rs = sem("stats_done"), sem("row_sd"), sem("row_rstd")
        row_g, row_g2, row_y, row_yp, out_rows = (sem(n) for n in ("row_gain", "row_scaled", "row_y", "row_y_pool", "out_rows"))

        class Chain:
            def __init__(self, eng, s):
                self.eng, self.s, self.n, self.base, self.stack = eng, s, 0, 0, []

            def __call__(self, ins):
                ins.then_inc(self.s, 1)
                self.n += 1
                self.eng.wait_ge(self.s, self.base + self.n)

            def enter(self, i, per, times):
                self.stack.append((self.n, self.base, per, times))
                self.base, self.n = i * per + (self.base + self.n), 0

            def leave(self):
                n, base, per, times = self.stack.pop()
                assert self.n == per, (self.n, per)
                self.n, self.base = n + per * times, base

        def one(t, k):
            return t[:, bass.ds(k, 1), :].rearrange("p a c -> p (a c)")

        def settle(eng):
            eng.sem_inc(settled, 1)

        def flat(t):
            return t[:, :, :].rearrange("p k c -> p (k c)")

        def one_dram(t, k):
            return t[bass.ds(k, 1), :, :].rearrange("a p c -> (a p) c")

        def cache_head(t, h):
            return t.rearrange("(j p) h d -> p j h d", p=128)[:, :, bass.ds(h, 1), :].rearrange("p j a d -> p j (a d)")

        def row_head(t, h):
            return t[:, bass.ds(h, 1), :].rearrange("t a d -> t (a d)")

        def tile_s(i, n):
            return S[0:n, S_OFF[i]:S_OFF[i] + S_LEN[i]]

        def gate2(t):
            return t[:, :].rearrange("p (h c) -> p h c", h=2)

        def done(m, G, s, C):
            return (unit_done, G * 2 + (s + 3)) if m else (m0_done, C + 1)

        def free(m, C):
            return ev[m], C + (1 + SHIFT[m])

        def pair(m, rows=128):
            return PS[0:rows, 2 * m:2 * m + 2, 0:HALF]

        def halves(ap):
            return ap.rearrange("p (h c) -> p h c", h=2)

        w_view = {n: w.rearrange("(k p) c -> p k c", p=128)
                  for n, w in (("in", w_in), ("out", w_out), ("up", w_up), ("down", w_down))}
        w_f = w_in.rearrange("(k p) c -> p k c", p=128)[:, :, F_COL:F_COL + NH]
        raw_f = RAW[1][:, :, :].rearrange("p k c -> p (k c)").rearrange("p (k c) -> p k c", k=KT)
        wh_f = WH[1][:, :, :].rearrange("p k c -> p (k c)").rearrange("p (k c) -> p k c", k=KT)
        wl_f = WL[1][:, :, :].rearrange("p k c -> p (k c)").rearrange("p (k c) -> p k c", k=KT)

        def load(sp, u, s, src):
            sp.wait_ge(lo_done, u)
            sp.dma_start(RAW[s][:, :, :], src).then_inc(raw_in[s], 16)

        def load_group(sp, G, srcs):
            for s in range(2):
                load(sp, G * 2 + (s + 1), s, srcs[s])

        def hi(act, G, s):
            act.wait_ge(raw_in[s], G * 16 + 16 * (s + 1))
            act.wait_ge(unit_done, G * 2 + (s + 1))
            act.activation(WH[s][:, :, :], RAW[s][:, :, :], ACT.Copy).then_inc(hi_done, 1)

        def lo(dve, G, s):
            dve.wait_ge(hi_done, G * 2 + (s + 2))
            dve.tensor_tensor(WL[s][:, :, :], RAW[s][:, :, :], WH[s][:, :, :].bitcast(F32),
                              ALU.subtract).then_inc(lo_done, 1)

        def products(pe, m, s, k, kk, X, Y, first, final, to=None):
            to = m if to is None else to
            a, b = WH[s][:, k, 128 * m:128 * m + 128], WL[s][:, k, 128 * m:128 * m + 128]
            last_mm = None
            for n, (w, x) in enumerate(((a, X), (a, Y), (b, X))):
                for h, c in ((0, HALF), (1, X.shape[-1] - HALF)):
                    last_mm = pe.matmul(PS[:, 2 * to + h, 0:c], w, x[:, kk, HALF * h:HALF * h + c],
                                        start=(first and n == 0), stop=(final and n == 2))
            return last_mm

        def group(pe, G, frees, X, Y, after_a=None):
            for s in range(2):
                pe.wait_ge(lo_done, G * 2 + (s + 3))
                for m in range(2):
                    if s == 0:
                        pe.wait_ge(*frees[m])
                    for k in range(UK):
                        kk = UK * s + k
                        mm = products(pe, m, s, k, kk, X, Y, kk == 0, kk == KT - 1)
                    if m == 1:
                        mm.then_inc(unit_done, 1)
                    elif s == 1:
                        mm.then_inc(m0_done, 1)
                if s == 0 and after_a is not None:
                    after_a()

        def narrow(pe, G, s, C, X, Y, k0, ready=None, at=0):
            pe.wait_ge(lo_done, G * 2 + (s + 3))
            for m in range(2):
                pe.wait_ge(*free(m, C))
                for k in range(UK):
                    if ready is not None and s == 0 and m == 0:
                        pe.wait_ge(ready, at + (k + 1))
                    mm = products(pe, m, s, k, k0 + k, X, Y, k == 0, k == UK - 1)
                mm.then_inc(unit_done if m else m0_done, 1)

        block = ctx.enter_context(nc.Block())

        @block.sync
        def _(sp):
            for p in range(2):
                c = slice(D // 2 * p, D // 2 * (p + 1))
                for t in range(4):
                    sp.dma_start(XROW[:, t, c], x_prompt[128 * t:128 * t + 128, c]).then_inc(x_in[p], 16)
                sp.dma_start(XROWS[:, c], x_sample[:, c]).then_inc(x_in[p], 16)
            sp.wait_ge(cf_clear, 1)
            with nc.allow_non_contiguous_dma(reason="4 columns"):
                sp.dma_start(raw_f[:, :, 0:NH], w_f).then_inc(raw_in[1], 16)
            with sp.Fori(0, 20) as i:
                load_group(sp, i, [w_view["in"][:, UK * s:UK * s + UK, bass.ds(i * UC, UC)] for s in range(2)])
            load_group(sp, G_O1, [w_view["out"][:, 0:UK, UC * s:UC * s + UC] for s in range(2)])
            for m in range(2):
                sp.wait_ge(stg_out[m], 16 * 13)
            sp.wait_ge(ss_done, NA)
            sp.wait_ge(last_a, 2 * (CONV - 1))
            sp.wait_ge(fd_out, 32)

            def load_heads(q, it, kc, vc):
                for par in range(2):
                    hc = it * 2 + (4 * q + par)
                    h = it * 2 + par
                    sp.wait_ge(pv_done, hc + 1)
                    for dst, n in ((QF, 0), (KF, 1), (VF, 2)):
                        sp.dma_start(dst[par][:, :], one_dram(QS, h + NH * (3 * q + n))).then_inc(att_in[par], 16)
                    sp.dma_start(VC[par][:, :, :], cache_head(vc, h)).then_inc(att_in[par], 16)
                    sp.wait_ge(tp, hc * 4 + 1)
                    sp.dma_start(KC[:, :, :], cache_head(kc, h)).then_inc(att_in[par], 16)
                    x = it * 2 + (4 * q + par + 2)
                    rows, x = (slice(0, UK), x) if not isinstance(x, int) or x < 8 else (slice(UK, 2 * UK), x - 8)
                    load(sp, hc + (2 * G_O1 + 3), par, w_view["out"][:, rows, bass.ds(x * UC, UC)])
                    if q:
                        sp.wait_ge(bf_done, h * 5 + 1)
                        f = FD[bass.ds(h, 1), :]
                        sp.dma_start(FB[:, :], f.to_broadcast([128, SEQ + PAST + DEC])).then_inc(fb_in, 16)

            with sp.Fori(0, 2) as it:
                load_heads(0, it, band_k, band_v)
            for it in range(2):
                load_heads(1, it, fox_k, fox_v)

            def load_narrow(name, G, j, k0):
                load_group(sp, G, [w_view[name][:, k0, bass.ds(j * 2 * UC + UC * s, UC)] for s in range(2)])

            def load_up(G, j, col):
                load_group(sp, G, [w_view["up"][:, UK * s:UK * s + UK, bass.ds(j * UC + col, UC)] for s in range(2)])

            with sp.Fori(1, 4) as j:
                load_narrow("out", j + G_O2, j, slice(UK, 2 * UK))
            with sp.Fori(0, 4) as j:
                load_up(j + G_U0, j, 0)
            with sp.Fori(0, 4) as j:
                load_narrow("down", j + G_D0, j, slice(0, UK))
            with sp.Fori(0, MID) as c:
                with sp.Fori(0, 4) as j:
                    load_up(c * 8 + j + G_C, j, c * (UC * 4) + UC * 4)
                with sp.Fori(0, 4) as j:
                    load_narrow("down", c * 8 + j + (G_C + 4), j, bass.ds(c * UK + UK, UK))
            with sp.Fori(0, 4) as j:
                load_up(j + G_U7, j, UC * 4 * (N_CHUNK - 1))
            with sp.Fori(0, 4) as j:
                load_narrow("down", j + G_D7, j, slice(UK * (N_CHUNK - 1), UK * N_CHUNK))
            for done_, n, t in ((row_yp, 1, 0), (row_y, 1, 2), (row_yp, 2, 1), (row_y, 2, 3), (row_y, 3, 4)):
                sp.wait_ge(done_, n)
                dst, src = (y_prompt[128 * t:128 * t + 128, :], ROWS[:, t, :]) if t < 4 else (y_sample, ROW_S[:, :])
                sp.dma_start(dst, src).then_inc(out_rows, 16)
            sp.wait_ge(out_rows, 16 * TT)
            sp.wait_ge(stores, 16 * 6)
            for p in range(2):
                sp.wait_ge(kv_out[p], 64 * 5)

        @block.scalar
        def _(act):
            chain = Chain(act, act_c)
            rows = [(VR1, 0, g_mix), (VR1, 16, ln1_g), (VR1, 32, ln1_b),
                    (VR1, 48, w_conv), (VR1, 80, b_conv), (VR1, 88, b_ra),
                    (VR2, 0, b_rx), (VR2, 8, lam), (VR2, 16, state_lru), (VR2, 24, state_conv)]
            for dst, at, src in rows:
                v = src.rearrange("a (t p) -> (a t) p", p=128)
                act.dma_start(dst[at:at + v.shape[0], :], v).then_inc(vec_in, 16)
            act.dma_start(CFL[:, :, :], fox_logf.rearrange("(j p) h -> p j h", p=128)).then_inc(vec_in, 16)
            with nc.allow_non_contiguous_dma(reason="4 numbers"):
                act.dma_start(tiny[0:NH, 0:1], b_forget.rearrange("a h -> h a")).then_inc(vec_in, 16)
            for k in range(KT):
                act.wait_ge(xt_done, k + 1)
                act.activation(XH[:, k, :], PSF[:, 1024 * (k % 4):1024 * (k % 4) + TOK], ACT.Copy).then_inc(xh_done, 1)
            act.wait_ge(raw_in[1], 16)
            act.activation(WH[1][:, :, :], RAW[1][:, :, :], ACT.Copy).then_inc(hi_done, 1)
            act.wait_ge(vec_t, 1)
            act.activation(VT1[:, :], PS[:, 4, 0:96], ACT.Copy).then_inc(vec_done, 1)
            act.activation(VT2[:, :], PS[:, 5, 0:48], ACT.Copy).then_inc(vec_done, 1)
            act.activation(CL[:, :], PS[0:NH, 6, :], ACT.Copy).then_inc(vec_done, 1)
            hi(act, 0, 0)
            act.wait_ge(unit_done, 2)
            act.activation(halves(ZT[:, :]), pair(1, NH), ACT.Identity, bias=tiny[0:NH, 0:1]).then_inc(ev[1], 1)
            hi(act, 0, 1)
            act.wait_ge(vec_done, 3)
            act.wait_ge(ev[1], 1)
            chain(act.activation(ZA[:, :], ZT[:, :], ACT.Abs))
            chain(act.activation(LZ[:, 0, :], VT2[:, 8:16], ACT.Abs))
            chain(act.activation(ZA[:, :], ZA[:, :], ACT.Exp, scale=-1.0))
            act.activation(LZ[:, 0, :], LZ[:, 0, :], ACT.Exp, scale=-1.0).then_inc(z_exp, 1)
            act.wait_ge(z_u, 2)
            act.activation(ZC[:, :], ZB[:, :], ACT.Ln).then_inc(z_ln, 1)
            act.activation(LZ[:, 2, :], LZ[:, 1, :], ACT.Ln).then_inc(z_ln, 1)
            act.wait_ge(ext_out, 16)
            act.wait_ge(xl_done, KT)

            def evac_x(m, i):
                act.wait_ge(*done(m, i + G_A, 1, i + G_A))
                t = i * 2 + m
                act.activation(one(XA, t)[:, CONV - 1:CONV - 1 + HALF], PS[:, 2 * m, 0:HALF], ACT.Copy)
                act.activation(one(XA, t)[:, CONV - 1 + HALF:CONV - 1 + SEQ], PS[:, 2 * m + 1, 0:SEQ - HALF], ACT.Copy)
                act.activation(one(XA, t)[:, S_AT + 3:S_AT + 3 + DEC], PS[:, 2 * m + 1, SEQ - HALF:HALF],
                               ACT.Copy).then_inc(ev[m], 1)

            with act.Fori(0, 4) as i:
                hi(act, i + (G_A + 1), 0)
                evac_x(0, i)
                evac_x(1, i)
                hi(act, i + (G_A + 1), 1)
            with act.Fori(0, 4) as i:
                hi(act, i + (G_A + 5), 0)
                for m in range(2):
                    act.wait_ge(*done(m, i + (G_A + 4), 1, i + (G_A + 4)))
                    act.activation(halves(one(YF, i * 2 + m)), pair(m), ACT.Copy).then_inc(ev[m], 1)
                hi(act, i + (G_A + 5), 1)
            act.wait_ge(ft_done, 1)
            chain(act.activation(LFT[:, 0:4, :], PS[:, 7, 0:16].rearrange("p (t h) -> p t h", h=NH), ACT.Copy))
            chain(act.activation(LFT[0:DEC, 4, :], PS[0:DEC, 7, 16:20], ACT.Copy))
            act.activation(FQ[:, 0:4, :], PS[:, 7, 20:36].rearrange("p (t h) -> p t h", h=NH), ACT.Copy).then_inc(ftc_done, 1)
            act.activation(FQ[0:DEC, 4, :], PS[0:DEC, 7, 36:40], ACT.Copy).then_inc(ftc_done, 1)
            act.dma_start(p_fl.rearrange("(t p) h -> p t h", p=128), LFT[:, 0:4, :]).then_inc(stores, 16)
            act.dma_start(s_fl, LFT[0:DEC, 4, :]).then_inc(stores, 16)

            def stage(m, i):
                act.wait_ge(*done(m, i + G_B, 1, i + G_B))
                act.wait_ge(stg_out[m], i * 16 + 16)
                act.activation(halves(STG[:, m, :]), pair(m), ACT.Copy).then_inc(ev[m], 1)
                act.wait_ge(ev[m], i + (G_B + 2))
                act.dma_start(one_dram(QS, i * 2 + m), STG[:, m, :]).then_inc(stg_out[m], 16)

            with act.Fori(0, NA) as i:
                act.dma_start(WRA[:, :], one_dram(w_ra, i)).then_inc(gw_in, 16)
                act.dma_start(WRX[:, :], one_dram(w_rx, i)).then_inc(gw_in, 16)
                hi(act, i + (G_B + 1), 0)
                chain.enter(i, 1, NA)
                act.wait_ge(gate_done, i + 1)
                chain(act.activation(gate2(TR), PS[:, 4:6, 0:CW // 2], ACT.Tanh, bias=half_b[:, 0, bass.ds(i, 1)], scale=0.5))
                act.activation(AA[:, :], TR[:, :], ACT.Exp, bias=c_sp[:, 0, bass.ds(i, 1)],
                               scale=c_sp[:, 0, bass.ds(i, 1)]).then_inc(a_done, 1)
                act.activation(T1[:, :], TR[:, :], ACT.Tanh, bias=c_sp[:, 1, bass.ds(i, 1)],
                               scale=c_sp[:, 1, bass.ds(i, 1)]).then_inc(a_done, 1)
                act.activation(gate2(TI), PS[:, 6:8, 0:CW // 2], ACT.Tanh, bias=half_b[:, 1, bass.ds(i, 1)],
                               scale=0.5).then_inc(ti_done, 1)
                act.wait_ge(gi_done, i + 1)
                act.activation(TH[:, :], GI[:, :], ACT.Tanh).then_inc(th_done, 1)
                stage(0, i)
                act.wait_ge(m2_done, i + 1)
                act.activation(T1[:, :], T1[:, :], ACT.Sqrt, scale=0.25).then_inc(sq_done, 1)
                stage(1, i)
                hi(act, i + (G_B + 1), 1)
                chain.leave()
            def plain(i):
                hi(act, i + (G_B + 1), 0)
                stage(0, i)
                stage(1, i)
                hi(act, i + (G_B + 1), 1)

            with act.Fori(NA, 10) as i:
                plain(i)
            act.wait_ge(ssa_mm, 1)
            act.activation(halves(SSA[:, :]), PS[:, 4:6, 0:HALF], ACT.Sqrt, bias=eps[:, :], scale=1.0 / DA).then_inc(ssa_sd, 1)
            with act.Fori(10, 12) as i:
                plain(i)

            act.wait_ge(unit_done, 2 * G_O1 + 2)
            for k in range(KT):
                act.activation(R[:, k, 0:TOK], XL[:, k, 0:TOK].bitcast(F32), ACT.Copy, scale=ALPHA).then_inc(r_alpha, 1)
                if 0 <= k - 2 < NA:
                    act.wait_ge(r_init, k - 1)
                    act.wait_ge(ya_done, k - 1)
                    act.activation(YH[:, k - 2, :], YF[:, k - 2, :], ACT.Copy).then_inc(yh_done, 1)
            act.wait_ge(r_init, KT)

            def head(q, it, par, out_k, out_v, new_k, new_v):
                hc = it * 2 + (4 * q + par)
                h = it * 2 + par
                act.wait_ge(tp, hc * 4 + 5)
                act.activation(KCT[:, :], PS[:, 6, :], ACT.Copy).then_inc(tc, 1)
                act.wait_ge(tp, hc * 4 + 6)
                act.wait_ge(kv_out[par], it * 64 + (128 * q + 64))
                act.activation(VT[par][:, 0:4, :], PS[:, 7, :].rearrange("p (j d) -> p j d", d=HD), ACT.Copy).then_inc(tc, 1)

                def new_rows():
                    act.wait_ge(tp, hc * 4 + 7)
                    act.activation(KTM[par][:, 0:4, :], PS[:, 6, :].rearrange("p (j d) -> p j d", d=HD), ACT.Copy).then_inc(tc, 1)
                    act.wait_ge(tp, hc * 4 + 8)
                    act.activation(VT[par][0:DEC, 4, :], PS[0:DEC, 7, 0:HD], ACT.Copy)
                    act.activation(KTM[par][0:DEC, 4, :], PS[0:DEC, 7, HD:2 * HD], ACT.Copy).then_inc(tc, 1)
                    act.wait_ge(tc, hc * 4 + 4)
                    for dst, src in ((cache_head(out_k, h), KTM[par][:, 0:4, :]), (cache_head(out_v, h), VT[par][:, 0:4, :]),
                                     (row_head(new_k, h), KTM[par][0:DEC, 4, :]), (row_head(new_v, h), VT[par][0:DEC, 4, :])):
                        act.dma_start(dst, src).then_inc(kv_out[par], 16)

                def exp(i):
                    n = DEC if i == 4 else 128
                    act.wait_ge(mx, hc * 5 + (i + 1))
                    act.activation(tile_s(i, n), tile_s(i, n), ACT.Exp, bias=small[0:n, i, 0:1],
                                   accum_out=small[0:n, i, 1:2]).then_inc(ex, 1)

                def copy_pt(i):
                    act.wait_ge(pt, hc * 5 + (i + 1))
                    b = 6 + i % 2
                    if i < 4:
                        act.activation(PT[:, 0:i + 1, 128 * i:128 * i + 128],
                                       PS[:, b, 0:128 * (i + 1)].rearrange("p (j c) -> p j c", c=128), ACT.Copy).then_inc(ptc, 1)
                    else:
                        act.activation(PTS[:, 0:4, :], PS[:, b, 0:4 * DEC].rearrange("p (j c) -> p j c", c=DEC), ACT.Copy)
                        act.activation(PTS[0:DEC, 4, :], PS[0:DEC, b, 4 * DEC:5 * DEC], ACT.Copy).then_inc(ptc, 1)

                exp(0)
                exp(1)
                new_rows()
                for i in range(2, 5):
                    exp(i)
                for i in range(5):
                    copy_pt(i)
                act.wait_ge(pv_done, hc + 3)
                act.activation(one(YF, h + (NA + NH * q)), PSF[:, 2048:2048 + TOK], ACT.Copy).then_inc(yv, 1)
                hi(act, it + (G_O1 + 1 + 2 * q), par)

            with act.Fori(0, 2) as it:
                for par in range(2):
                    head(0, it, par, p_bk, p_bv, s_bk, s_bv)
            with act.Fori(0, 2) as it:
                for par in range(2):
                    head(1, it, par, p_fk, p_fv, s_fk, s_fv)

            act.wait_ge(yv, 9)
            act.wait_ge(mx, 40)
            for t in range(8):
                a = t - t // NH - 1
                if t % NH and a >= 2:
                    act.wait_ge(yss, a - 1)
                dst = (Q2, Q3)[a % 2] if t % NH else (Q0, Q1)[t // NH]
                act.activation(dst[:, :], YF[:, NA + t, :], ACT.Square).then_inc(ysq, 1)
            for q, n in enumerate((Q0, Q1)):
                act.wait_ge(y_mm, q + 1)
                act.activation(halves(n[:, :]), PS[:, 2 + 2 * q:4 + 2 * q, 0:HALF], ACT.Sqrt, bias=eps[:, :],
                               scale=1.0 / (NH * HD)).then_inc(y_sd, 1)
            for k in range(NA, KT):
                act.wait_ge(y_g, k - NA + 1)
                act.activation(YH[:, k, :], YF[:, k, :], ACT.Copy).then_inc(yh_done, 1)
            act.wait_ge(last_t, 1)
            act.activation(LROW[:, :], PS[0:64, 6, 0:128], ACT.Copy).then_inc(last_c, 1)
            act.wait_ge(last_c, 1)
            for at, dst in ((0, p_conv), (24, s_conv), (48, p_lru), (56, s_lru)):
                v = dst.rearrange("a (t p) -> (a t) p", p=128)
                act.dma_start(v, LROW[at:at + v.shape[0], :]).then_inc(stores, 16)

            with act.Fori(0, 4) as j:
                for s in range(2):
                    hi(act, j + (G_O2 + 1), s)
            act.wait_ge(unit_done, 2 * G_U0 + 2)
            for c in range(2):
                act.activation(X1H[:, :, TOK + c], L1B, ACT.Copy).then_inc(b_hi, 1)
            act.activation(alpha_b[:, :], L1B, ACT.Copy, scale=ALPHA)
            for k in range(KT):
                act.wait_ge(ln_xc, k + 1)
                act.activation(X1H[:, k, 0:TOK], R[:, k, 0:TOK], ACT.Identity, scale=L1G[:, k:k + 1]).then_inc(x1h_done, 1)
                if k >= 3:
                    act.wait_ge(ln_ss, k - 2)
                act.activation(NQ[k % 3][:, :], R[:, k, 0:TOK], ACT.Square).then_inc(ln_sq, 1)
                if k == 11:
                    hi(act, G_U0 + 1, 0)
            for p in range(2):
                act.wait_ge(kv_out[p], 64 * 5)

            def relu2(m, t, C):
                act.wait_ge(ev[m], C + (2 + SHIFT[m]))
                chain(act.activation(RT[m][:, :], RT[m][:, :], ACT.Relu, bias=wb[:, m:m + 1]))
                chain(act.activation(RT[m][:, :], RT[m][:, :], ACT.Square))
                act.activation(one(HHI, t), RT[m][:, :], ACT.Copy).then_inc(hh_done, 1)

            for j in range(4):
                if j:
                    hi(act, G_U0 + j + 1, 0)
                else:
                    hi(act, G_U0 + 1, 1)
                    act.wait_ge(ln_mm2, 1)
                    act.activation(halves(ND[:, :]), pair(3), ACT.Sqrt, bias=eps[:, :], scale=1.0 / D).then_inc(ln_sd, 1)
                for m in range(2):
                    relu2(m, 2 * j + m, C_U0 + j)
                if j >= 2:
                    for k in range(8 * (j - 2), 8 * (j - 1)):
                        act.wait_ge(acc_mul, k + 1)
                        act.activation(ACC[:, k, :], ACC[:, k, :], ACT.Identity, bias=alpha_b[:, k:k + 1], scale=ALPHA)\
                           .then_inc(acc_init, 1)
                if j:
                    hi(act, G_U0 + j + 1, 1)

            def down(G):
                with act.Fori(0, 4) as j:
                    for s in range(2):
                        hi(act, j + (G + 1), s)

            def up(G, C):
                with act.Fori(0, 4) as j:
                    chain.enter(j, 4, 4)
                    hi(act, G + j + 1, 0)
                    for m in range(2):
                        relu2(m, j * 2 + m, C + j)
                    hi(act, G + j + 1, 1)
                    chain.leave()

            down(G_D0)
            with act.Fori(0, MID) as c:
                chain.enter(c, 16, MID)
                up(c * 8 + G_C, c * 12 + C_C)
                down(c * 8 + (G_C + 4))
                chain.leave()
            up(G_U7, C_U7)

            def rows_copy(u):
                c = slice(UC * u, UC * u + UC)
                for q, (dst, src) in enumerate(((ROWS[:, 0:2, c], PS[:, 4, :].rearrange("p (q c) -> p q c", q=2)),
                                                (ROWS[:, 2:4, c], PS[:, 5, :].rearrange("p (q c) -> p q c", q=2)),
                                                (ROW_S[:, c], PS[0:DEC, 6, 0:UC]))):
                    act.wait_ge(rows_t, 3 * u + q + 1)
                    act.activation(dst, src, ACT.Copy).then_inc(rows_c, 1)

            for u in range(8):
                if u < 6:
                    hi(act, G_D7 + u // 2 + 1, u % 2)
                if u:
                    rows_copy(u - 1)
            rows_copy(7)
            act.wait_ge(stats_done, 1)
            act.activation(RST[:, 0:4], MV[:, 0:4, 1], ACT.Sqrt, bias=eps[:, :]).then_inc(row_sd, 1)
            act.activation(RST[0:DEC, 4:5], MV[0:DEC, 4, 1:2], ACT.Sqrt, bias=eps[0:DEC, :]).then_inc(row_sd, 1)
            act.wait_ge(row_rs, 1)
            for t in range(2):
                act.wait_ge(row_g, t + 1)
                act.activation(ROWS[:, t, :], ROWS[:, t, :], ACT.Copy, scale=RST[:, t:t + 1]).then_inc(row_g2, 1)

        @block.vector
        def _(dve):
            chain = Chain(dve, dve_c)
            for s, n in ((lo_done, 1), (unit_done, 1), (ev[0], 1), (stg_out[0], 16), (stg_out[1], 16), (kv_out[0], 64),
                         (kv_out[1], 64), (pv_done, 2), (yv, 1), (tp, 4), (bf_done, 1)):
                dve.sem_inc(s, n)
            chain(dve.memset(eps[:, :], EPS))
            dve.wait_ge(rel_in, 16)
            chain(dve.tensor_copy(EXT[:, 0:REV], REL[:, NREL - 1:NREL].to_broadcast([NH, REV])))
            dve.tensor_copy(EXT[:, REV:EW], REL[:, NREL - (EW - REV):NREL][:, ::-1]).then_inc(ext_done, 1)
            for k in range(KT):
                dve.wait_ge(xh_done, k + 1)
                dve.tensor_tensor(XL[:, k, 0:TOK], PSF[:, 1024 * (k % 4):1024 * (k % 4) + TOK], XH[:, k, :].bitcast(F32),
                                  ALU.subtract).then_inc(xl_done, 1)
            dve.wait_ge(hi_done, 1)
            dve.tensor_tensor(WL[1][:, :, :], RAW[1][:, :, :], WH[1][:, :, :].bitcast(F32), ALU.subtract).then_inc(lo_done, 1)
            lo(dve, 0, 0)
            dve.wait_ge(vec_done, 2)
            chain(dve.tensor_scalar(half_b[:, 0, :], VT1[:, 88:96], 0.5, None, ALU.mult))
            chain(dve.tensor_scalar(half_b[:, 1, :], VT2[:, 0:8], 0.5, None, ALU.mult))
            lo(dve, 0, 1)
            dve.wait_ge(z_exp, 1)
            cases = ((ZT[:, :], ZA[:, :], ZB[:, :], ZC[:, :], ZT[:, :]),
                     (VT2[:, 8:16], LZ[:, 0, :], LZ[:, 1, :], LZ[:, 2, :], LZ[:, 3, :]))
            for z, e, u, ln, out in cases:
                dve.tensor_scalar(u, e, 1.0, None, ALU.add).then_inc(z_u, 1)
            dve.wait_ge(z_ln, 2)
            for z, e, u, ln, out in cases:
                chain(dve.tensor_scalar(u, u, 1.0, None, ALU.subtract))
                chain(dve.scalar_tensor_tensor(ln, u, 0.0, ln, ALU.is_equal, ALU.add))
                chain(dve.scalar_tensor_tensor(u, u, 0.0, u, ALU.is_equal, ALU.add))
                chain(dve.reciprocal(u, u))
                chain(dve.tensor_tensor(u, u, e, ALU.mult))
                chain(dve.tensor_tensor(ln, ln, u, ALU.mult))
                chain(dve.scalar_tensor_tensor(out, z, 0.0, ln, ALU.min, ALU.subtract))
            chain(dve.tensor_scalar(c_sp[:, 0, :], LZ[:, 3, :], 4.0, None, ALU.mult))
            chain(dve.tensor_scalar(c_sp[:, 1, :], LZ[:, 3, :], -4.0, None, ALU.mult))
            dve.wait_ge(vec_done, 3)
            chain(dve.memset(ZB[:, :], 1.0))
            chain(dve.tensor_tensor_scan(FP[:, 0:SEQ], ZB[:, 0:SEQ], ZT[:, 0:SEQ], 0.0, ALU.mult, ALU.add))
            chain(dve.tensor_tensor_scan(FS[:, 0:PAST], ZB[:, 0:PAST], CL[:, :], 0.0, ALU.mult, ALU.add))
            dve.tensor_tensor_scan(FS[:, PAST:], ZB[:, 0:DEC], ZT[:, SEQ:], FS[:, PAST - 1:PAST], ALU.mult, ALU.add)\
               .then_inc(f_done, 1)
            with dve.Fori(0, 8) as i:
                for s in range(2):
                    lo(dve, i + (G_A + 1), s)
            dve.wait_ge(xa_init, CONV - 1)
            dve.wait_ge(ev[0], 9)
            dve.wait_ge(ev[1], 9)
            dve.wait_ge(ft_done, 1)
            with dve.Fori(0, NA) as i:
                chain.enter(i, 6, NA)
                xa, g = one(XA, i), one(YF, i)

                def tap(j):
                    return WC[:, bass.ds(i + 8 * j, 1)]

                chain(dve.tensor_scalar(XC[:, :], xa[:, 0:CW], tap(0), BC[:, bass.ds(i, 1)], ALU.mult, ALU.add))
                for j in range(1, CONV - 1):
                    chain(dve.scalar_tensor_tensor(XC[:, :], xa[:, j:j + CW], tap(j), XC[:, :], ALU.mult, ALU.add))
                j = CONV - 1
                dve.scalar_tensor_tensor(XC[:, :], xa[:, j:j + CW], tap(j), XC[:, :], ALU.mult, ALU.add).then_inc(conv_done, 1)
                lo(dve, i + (G_B + 1), 0)
                dve.wait_ge(ti_done, i + 1)
                chain(dve.scalar_tensor_tensor(UX[:, :], TI[:, :], 1.0, XC[:, :], ALU.add, ALU.mult))
                dve.wait_ge(a2_done, i + 1)
                dve.scalar_tensor_tensor(T1[:, :], HS[:, :], 1.0, T1[:, :], ALU.add, ALU.mult).then_inc(m2_done, 1)
                dve.wait_ge(th_done, i + 1)
                dve.scalar_tensor_tensor(GG[:, :], TH[:, :], 1.0, g, ALU.add, ALU.mult)
                dve.wait_ge(sq_fix, i + 1)
                chain(dve.tensor_tensor(UX[:, :], UX[:, :], T1[:, :], ALU.mult))
                dve.tensor_tensor_scan(HS[:, 0:SEQ], AA[:, 0:SEQ], UX[:, 0:SEQ], 0.0, ALU.mult, ALU.add)
                chain(dve.tensor_tensor_scan(HS[:, SEQ:TOK], AA[:, S_AT:S_AT + DEC], UX[:, S_AT:S_AT + DEC],
                                             H0[:, bass.ds(i, 1)], ALU.mult, ALU.add))
                dve.scalar_tensor_tensor(g, HS[:, 0:TOK], 0.5, GG[:, :], ALU.mult, ALU.mult).then_inc(y_done, 1)
                lo(dve, i + (G_B + 1), 1)
                chain.leave()
            with dve.Fori(NA, 10) as i:
                for s in range(2):
                    lo(dve, i + (G_B + 1), s)
            dve.wait_ge(ssa_sd, 1)
            chain(dve.reciprocal(SSA[:, :], SSA[:, :]))
            for k in range(NA):
                dve.scalar_tensor_tensor(YF[:, k, :], YF[:, k, :], GM[:, k:k + 1], SSA[:, :], ALU.mult, ALU.mult).then_inc(ya_done, 1)
            with dve.Fori(10, 12) as i:
                for s in range(2):
                    lo(dve, i + (G_B + 1), s)
            for k in range(KT):
                dve.wait_ge(r_alpha, k + 1)
                dve.scalar_tensor_tensor(R[:, k, 0:TOK], XH[:, k, :].bitcast(F32), ALPHA, R[:, k, 0:TOK], ALU.mult, ALU.add).then_inc(r_init, 1)
                if 0 <= k - 2 < NA:
                    dve.wait_ge(yh_done, k - 1)
                    dve.tensor_tensor(YL[:, k - 2, :], YF[:, k - 2, :], YH[:, k - 2, :].bitcast(F32), ALU.subtract).then_inc(y_ready, 1)
            dve.wait_ge(r_init, KT)
            dve.wait_ge(m_done, 1)

            def head(q, it, par):
                hc = it * 2 + (4 * q + par)
                h = it * 2 + par
                chain.enter(it, 20, 2) if par == 0 else None

                def score(i):
                    n = DEC if i == 4 else 128
                    dve.wait_ge(sc, hc * 5 + (i + 1))
                    if q:
                        dve.wait_ge(bf_done, it * 10 + (5 * par + i + 2))
                        bias = BF[0:n, S_OFF[i]:S_OFF[i] + S_LEN[i]]
                    else:
                        at = 0 if i == 4 else 512 - 128 * i
                        bias = one(M, h)[0:n, at:at + S_LEN[i]]
                    src = PSF[0:n, 2048:2048 + TOK] if i == 4 else PS[:, 2 + i % 2, 0:S_LEN[i]]
                    chain(dve.scalar_tensor_tensor(tile_s(i, n), src, SCALE, bias, ALU.mult, ALU.add))
                    dve.tensor_reduce(small[0:n, i, 0:1], tile_s(i, n), AX.X, ALU.max, negate=True).then_inc(mx, 1)

                def normalise(i):
                    n = DEC if i == 4 else 128
                    dve.wait_ge(ex, hc * 5 + (i + 1))
                    chain(dve.reciprocal(small[0:n, i, 2:3], small[0:n, i, 1:2]))
                    dve.tensor_scalar(tile_s(i, n), tile_s(i, n), small[0:n, i, 2:3], None, ALU.mult).then_inc(pn, 1)

                def project(m):
                    G, C = it + (G_O1 + 2 * q), it * 2 + (C_O1 + 4 * q + par)
                    dve.wait_ge(*done(m, G, par, C))
                    t = halves(one(R, hc * 2 + m)[:, 0:TOK])
                    dve.tensor_tensor(t, pair(0), t, ALU.add).then_inc(ev[0], 1)

                score(0)
                score(1)
                score(2)
                normalise(0)
                score(3)
                normalise(1)
                score(4)
                project(0)
                for i in range(2, 5):
                    normalise(i)
                project(1)
                lo(dve, it + (G_O1 + 1 + 2 * q), par)
                if par == 1:
                    chain.leave()

            for q in range(2):
                with dve.Fori(0, 2) as it:
                    for par in range(2):
                        head(q, it, par)
            for t in range(8):
                if t % NH:
                    a, n = t - t // NH - 1, (Q0, Q1)[t // NH]
                    dve.wait_ge(ysq, t + 1)
                    dve.tensor_tensor(n[:, :], n[:, :], (Q2, Q3)[a % 2][:, :], ALU.add).then_inc(yss, 1)
                    dve.wait_ge(yss, a + 1)

            def y_lo(k):
                dve.wait_ge(yh_done, k + 1)
                dve.tensor_tensor(YL[:, k, :], YF[:, k, :], YH[:, k, :].bitcast(F32), ALU.subtract).then_inc(y_ready, 1)

            for k in range(NA, KT):
                q, n = (k - NA) // NH, (Q0, Q1)[(k - NA) // NH]
                if (k - NA) % NH == 0:
                    dve.wait_ge(y_sd, q + 1)
                    chain(dve.reciprocal(n[:, :], n[:, :]))
                dve.scalar_tensor_tensor(YF[:, k, :], YF[:, k, :], GM[:, k:k + 1], n[:, :], ALU.mult, ALU.mult).then_inc(y_g, 1)
                if k > NA:
                    y_lo(k - 1)
            y_lo(KT - 1)

            def add_tile(T, t, m, G, s, C):
                dve.wait_ge(*done(m, G, s, C))
                at = halves(one(T, t)[:, 0:TOK])
                dve.tensor_tensor(at, pair(m), at, ALU.add).then_inc(ev[m], 1)

            with dve.Fori(0, 4) as j:
                for s in range(2):
                    for m in range(2):
                        add_tile(R, j * 4 + (2 * s + m), m, j + G_O2, s, j * 2 + (C_O2 + s))
                    lo(dve, j + (G_O2 + 1), s)
            dve.wait_ge(b_hi, 2)
            for c in range(2):
                dve.tensor_tensor(X1L[:, :, TOK + c], L1B, X1H[:, :, TOK + c].bitcast(F32), ALU.subtract)

            def x1_lo(k):
                dve.wait_ge(x1h_done, k + 1)
                dve.wait_ge(ln_sq, k + 1)
                dve.scalar_tensor_tensor(X1L[:, k, 0:TOK], R[:, k, 0:TOK], L1G[:, k:k + 1], X1H[:, k, 0:TOK].bitcast(F32),
                                         ALU.mult, ALU.subtract).then_inc(x1_ready, 1)

            dve.wait_ge(ln_mm1, 1)
            for m in range(2):
                dve.wait_ge(ev[m], C_U0 + 1 + SHIFT[m])
            for k in range(KT + 2):
                if k < KT:
                    t = halves(R[:, k, 0:TOK])
                    dve.scalar_tensor_tensor(t, pair(2), -1.0 / D, t, ALU.mult, ALU.add).then_inc(ln_xc, 1)
                if k >= 2:
                    x1_lo(k - 2)
                if k == 13:
                    lo(dve, G_U0 + 1, 0)
            for p in range(2):
                dve.wait_ge(kv_out[p], 64 * 5)

            def rescale(m, G, C, to, count):
                if not isinstance(count, int) or count >= 2:
                    dve.wait_ge(h_ready, count - 1)
                dve.wait_ge(*done(m, G, 1, C))
                dve.tensor_tensor(halves(RT[m][:, :]), pair(to), halves(RS[:, :]), ALU.mult)
                dve.tensor_copy(wb[:, m:m + 1], PS[:, 2 * to + 1, HALF:HALF + 1]).then_inc(ev[m], 1)

            def relu_lo(m, t, count):
                dve.wait_ge(hh_done, count + 1)
                dve.tensor_tensor(one(HLO, t), RT[m][:, :], one(HHI, t).bitcast(F32), ALU.subtract).then_inc(h_ready, 1)

            for j in range(4):
                if j:
                    lo(dve, G_U0 + j + 1, 0)
                else:
                    lo(dve, G_U0 + 1, 1)
                    dve.wait_ge(ln_sd, 1)
                    dve.reciprocal(RS[:, :], ND[:, :]).then_inc(ln_rs, 1)
                    dve.wait_ge(ln_rs, 1)
                for m in range(2):
                    rescale(m, G_U0 + j, C_U0 + j, m + 2 if j == 1 else m, 2 * j + m)
                for m in range(2):
                    relu_lo(m, 2 * j + m, 2 * j + m)
                if j:
                    lo(dve, G_U0 + j + 1, 1)

            def down(G, C):
                with dve.Fori(0, 4) as j:
                    for s in range(2):
                        for m in range(2):
                            add_tile(ACC, j * 4 + (2 * s + m), m, G + j, s, C + j * 2 + s)
                        lo(dve, G + j + 1, s)

            def up(c, G, C):
                with dve.Fori(0, 4) as j:
                    lo(dve, G + j + 1, 0)
                    rescale(0, G + j, C + j, 0, c * 8 + j * 2)
                    relu_lo(0, j * 2, c * 8 + j * 2)
                    rescale(1, G + j, C + j, 1, c * 8 + (j * 2 + 1))
                    relu_lo(1, j * 2 + 1, c * 8 + j * 2 + 1)
                    lo(dve, G + j + 1, 1)

            dve.wait_ge(acc_init, KT)
            down(G_D0, C_D0)
            with dve.Fori(0, MID) as c:
                up(c + 1, c * 8 + G_C, c * 12 + C_C)
                down(c * 8 + (G_C + 4), c * 12 + (C_C + 4))
            up(N_CHUNK - 1, G_U7, C_U7)

            def rows(t):
                return ROWS[:, t, :] if t < 4 else ROW_S[:, :]

            def n_rows(t):
                return 128 if t < 4 else DEC

            def row_stats(u):
                for t in range(TT):
                    dve.wait_ge(rows_c, 3 * u + t // 2 + 1)
                    st = dve.bn_stats(out=ST[0:n_rows(t), t, u, :], in_=rows(t)[:, UC * u:UC * u + UC])
                chain(st)

            for u in range(8):
                for m in range(2):
                    add_tile(ACC, 2 * u + m, m, G_D7 + u // 2, u % 2, C_D7 + u)
                if u < 6:
                    lo(dve, G_D7 + u // 2 + 1, u % 2)
                if u:
                    row_stats(u - 1)
            row_stats(7)
            for t in range(TT):
                mv = dve.bn_aggr(out=MV[0:n_rows(t), t, :], in_=ST[0:n_rows(t), t, :, :])
            mv.then_inc(stats_done, 1)
            dve.wait_ge(stats_done, 1)

            def gain(t):
                n = n_rows(t)
                return dve.scalar_tensor_tensor(rows(t), rows(t), MV[0:n, t, 0:1], GR[0:n, :], ALU.subtract, ALU.mult)

            dve.wait_ge(gb_in, 32)
            gain(0).then_inc(row_g, 1)
            dve.wait_ge(row_sd, 2)
            dve.reciprocal(RST[:, 0:4], RST[:, 0:4])
            dve.reciprocal(RST[0:DEC, 4:5], RST[0:DEC, 4:5]).then_inc(row_rs, 1)
            dve.wait_ge(row_rs, 1)
            gain(1).then_inc(row_g, 1)
            for t in range(2, TT):
                chain(gain(t))
                n = n_rows(t)
                dve.scalar_tensor_tensor(rows(t), rows(t), RST[0:n, t:t + 1], BR[0:n, :], ALU.mult, ALU.add).then_inc(row_y, 1)

        @block.gpsimd
        def _(pool):
            chain = Chain(pool, pool_c)
            pool.memset(raw_f, 0.0).then_inc(cf_clear, 1)
            chain(pool.memset(ident[:, :], 0.0))
            pool.affine_select(out=ident[:, :], in_=ident[:, :], compare_op=ALU.not_equal, fill=1.0, base=0,
                               pattern=[[-1, 128]], channel_multiplier=1).then_inc(const_done, 1)
            pool.memset(ones[:, :], 1.0).then_inc(const_done, 1)
            chain(pool.memset(sel[:, :, :], 0.0))
            pool.affine_select(out=sel[:, :, :], in_=sel[:, :, :], compare_op=ALU.not_equal, fill=1.0, base=0,
                               pattern=[[-1, NH], [0, 128]], channel_multiplier=1).then_inc(const_done, 1)
            pool.dma_start(REL[:, :], rel_bias).then_inc(rel_in, 16)
            pool.wait_ge(ext_done, 1)
            pool.dma_start(EXD, EXT[:, :]).then_inc(ext_out, 16)
            pool.wait_ge(ext_out, 16)
            for h in range(NH):
                pool.dma_start(REP[h], bass.AP(tensor=EXD.tensor, offset=EW * h, ap=[[0, 128], [1, EW]])).then_inc(rep_out, 16)
            pool.wait_ge(rep_out, 16 * NH)
            for h in range(NH):
                pool.dma_start(M[:, h, :], bass.AP(tensor=REP.tensor, offset=128 * EW * h + 127, ap=[[EW - 1, 128], [1, BW]]))\
                    .then_inc(m_in, 16)
            pool.wait_ge(xl_done, KT)
            pool.wait_ge(vec_done, 2)
            chain(pool.memset(XA[:, :, 0:CONV - 1], 0.0))
            chain(pool.memset(XA[:, :, XW - 2:XW], 0.0))
            chain(pool.memset(SSA[:, :], 0.0))
            for j in range(CONV - 1):
                pool.tensor_copy(XA[:, :, S_AT + j], SC[:, 8 * j:8 * j + 8]).then_inc(xa_init, 1)
            pool.wait_ge(m_in, 16 * NH)
            pool.memset(M[0:64, :, BW - 64:BW], NEG).then_inc(m_done, 1)
            pool.wait_ge(ev[0], 5)
            pool.wait_ge(ev[1], 5)
            for j in range(CONV - 1):
                pool.tensor_copy(last[:, 8 * j:8 * j + 8], XA[:, :, SEQ + j]).then_inc(last_a, 1)
                pool.tensor_copy(last[:, 24 + 8 * j:32 + 8 * j], XA[:, :, S_AT + DEC + j]).then_inc(last_a, 1)
            pool.wait_ge(ev[0], 9)
            pool.wait_ge(ev[1], 9)
            with pool.Fori(0, NA) as i:
                chain.enter(i, 5, NA)
                g = one(YF, i)
                chain(pool.tensor_tensor(GI[:, :], g, g, ALU.mult))
                settle(pool)
                chain(pool.tensor_scalar(GI[:, :], GI[:, :], GELU1, GELU0, ALU.mult, ALU.add))
                settle(pool)
                pool.tensor_tensor(GI[:, :], GI[:, :], g, ALU.mult).then_inc(gi_done, 1)
                pool.wait_ge(a_done, i * 2 + 2)
                settle(pool)
                pool.tensor_tensor(HS[:, :], AA[:, :], AA[:, :], ALU.mult).then_inc(a2_done, 1)
                pool.wait_ge(sq_done, i + 1)
                settle(pool)
                pool.memset(T1[:, 0:1], 0.5).then_inc(sq_fix, 1)
                pool.wait_ge(y_done, i + 1)
                settle(pool)
                chain(pool.tensor_copy(last[:, bass.ds(i + 48, 1)], HS[:, SEQ - 1:SEQ]))
                chain(pool.tensor_copy(last[:, bass.ds(i + 56, 1)], HS[:, TOK - 1:TOK]))
                settle(pool)
                chain(pool.tensor_tensor(GI[:, :], g, g, ALU.mult))
                settle(pool)
                pool.tensor_tensor(SSA[:, :], SSA[:, :], GI[:, :], ALU.add).then_inc(ss_done, 1)
                pool.wait_ge(ss_done, i + 1)
                chain.leave()
            pool.dma_start(FD[:, 0:SEQ], FP[:, 0:SEQ]).then_inc(fd_out, 16)
            pool.dma_start(FD[:, SEQ:], FS[:, :]).then_inc(fd_out, 16)
            pool.wait_ge(ftc_done, 2)

            for h in range(NH):
                pool.wait_ge(fb_in, 16 * (h + 1))
                for i in range(5):
                    n = DEC if i == 4 else 128
                    src = FB[0:n, SEQ:SEQ + PAST + DEC] if i == 4 else FB[:, 0:S_LEN[i]]
                    at = BF[0:n, S_OFF[i]:S_OFF[i] + S_LEN[i]]
                    diag = BF[0:n, S_OFF[i] + S_LEN[i] - n:S_OFF[i] + S_LEN[i]]
                    pool.wait_ge(mx, 5 * (h + NH - 1) + (i + 1 if h else 5))
                    chain(pool.tensor_scalar(at, src, -1.0, FQ[0:n, i, h:h + 1], ALU.mult, ALU.add))
                    pool.affine_select(out=diag, in_=diag, compare_op=ALU.is_ge, fill=NEG, base=0,
                                       pattern=[[-1, n]], channel_multiplier=1).then_inc(bf_done, 1)
            pool.wait_ge(pv_done, 10)
            for k in range(KT):
                pool.wait_ge(ev[k % 2], C_O2 + k // 2 + 2 + SHIFT[k % 2])
                if k == 0:
                    pool.tensor_copy(NS[:, :], R[:, 0, 0:TOK]).then_inc(ln_sum, 1)
                else:
                    pool.tensor_tensor(NS[:, :], NS[:, :], R[:, k, 0:TOK], ALU.add).then_inc(ln_sum, 1)
                pool.wait_ge(ln_sum, k + 1)
            pool.wait_ge(ln_mm1, 1)
            for k in range(KT):
                pool.wait_ge(ln_sq, k + 1)
                if k == 0:
                    pool.tensor_copy(NS[:, :], NQ[0][:, :]).then_inc(ln_ss, 1)
                else:
                    pool.tensor_tensor(NS[:, :], NS[:, :], NQ[k % 3][:, :], ALU.add).then_inc(ln_ss, 1)
                pool.wait_ge(ln_ss, k + 1)

            def times_gain(k):
                pool.wait_ge(x1_ready, k + 1)
                chain(pool.tensor_tensor(ACC[:, k, :], X1H[:, k, 0:TOK].bitcast(F32), X1L[:, k, 0:TOK].bitcast(F32), ALU.add))

            for k in range(3):
                times_gain(k)
            pool.wait_ge(ln_rs, 1)
            for k in range(KT):
                pool.tensor_tensor(ACC[:, k, :], ACC[:, k, :], RS[:, :], ALU.mult).then_inc(acc_mul, 1)
                if k + 3 < KT:
                    times_gain(k + 3)
            pool.wait_ge(unit_done, 2 * G_D7 + 2)
            pool.dma_start(GR[:, :], ln2_g.to_broadcast([128, D])).then_inc(gb_in, 16)
            pool.dma_start(BR[:, :], ln2_b.to_broadcast([128, D])).then_inc(gb_in, 16)
            pool.wait_ge(gb_in, 32)
            for t in range(2):
                pool.wait_ge(row_g2, t + 1)
                pool.tensor_tensor(ROWS[:, t, :], ROWS[:, t, :], BR[:, :], ALU.add).then_inc(row_yp, 1)

        @block.tensor
        def _(pe):
            pe.wait_ge(const_done, 3)
            for k in range(KT):
                if k % (KT // 2) == 0:
                    pe.wait_ge(x_in[k // (KT // 2)], 80)
                if k >= 4:
                    pe.wait_ge(xl_done, k - 3)
                b = 2 * (k % 4)
                for t in range(4):
                    pe.transpose(PS[:, b, 128 * t:128 * t + 128], XROW[:, t, 128 * k:128 * k + 128], ident[:, :])
                pe.transpose(PS[:, b + 1, 0:DEC], XROWS[:, 128 * k:128 * k + 128], ident[0:DEC, 0:DEC]).then_inc(xt_done, 1)
            pe.wait_ge(vec_in, 16 * 12)
            pe.wait_ge(xl_done, KT)
            pe.transpose(PS[:, 4, 0:96], VR1[:, :], ident[0:96, 0:96])
            pe.transpose(PS[:, 5, 0:48], VR2[:, :], ident[0:48, 0:48])
            for j in range(4):
                t = pe.transpose(PS[0:NH, 6, 128 * j:128 * j + 128], CFL[:, j, :], ident[:, :])
            t.then_inc(vec_t, 1)
            pe.wait_ge(lo_done, 2)
            n = 0
            for w, x in ((wh_f, XH), (wh_f, XL), (wl_f, XH)):
                for k in range(KT):
                    for h in range(2):
                        mm = pe.matmul(PS[:, 2 + h, 0:HALF], w[:, k, :], x[:, k, HALF * h:HALF * h + HALF],
                                       start=(n == 0), stop=(n == 3 * KT - 1))
                    n += 1
            mm.then_inc(unit_done, 1)
            with pe.Fori(0, 8) as i:
                group(pe, i + G_A, [(ev[m], i + (G_A + 1)) for m in range(2)], XH, XL)
            pe.wait_ge(f_done, 1)
            for t in range(4):
                pe.transpose(PS[:, 7, 4 * t:4 * t + 4], ZT[:, 128 * t:128 * t + 128], ident[0:NH, 0:NH])
                pe.transpose(PS[:, 7, 20 + 4 * t:24 + 4 * t], FP[:, 128 * t:128 * t + 128], ident[0:NH, 0:NH])
            pe.transpose(PS[0:DEC, 7, 16:20], ZT[:, SEQ:TOK], ident[0:NH, 0:NH])
            pe.transpose(PS[0:DEC, 7, 36:40], FS[:, PAST:PAST + DEC], ident[0:NH, 0:NH]).then_inc(ft_done, 1)
            pe.wait_ge(ftc_done, 2)
            with pe.Fori(0, NA) as i:
                def gates():
                    pe.wait_ge(gw_in, i * 32 + 32)
                    pe.wait_ge(conv_done, i + 1)
                    for b, w in ((4, WRA), (6, WRX)):
                        for h in range(2):
                            g = pe.matmul(PS[:, b + h, 0:CW // 2], w[:, :], XC[:, CW // 2 * h:CW // 2 * (h + 1)],
                                          start=True, stop=True)
                    g.then_inc(gate_done, 1)

                group(pe, i + G_B, [(ev[m], i + (G_B + 1)) for m in range(2)], XH, XL, after_a=gates)
            def plain(i):
                group(pe, i + G_B, [(ev[m], i + (G_B + 1)) for m in range(2)], XH, XL)

            with pe.Fori(NA, 10) as i:
                plain(i)
            pe.wait_ge(ss_done, NA)
            for h in range(2):
                mm = pe.matmul(PS[:, 4 + h, 0:HALF], ones[:, :], SSA[:, HALF * h:HALF * h + HALF], start=True, stop=True)
            mm.then_inc(ssa_mm, 1)
            with pe.Fori(10, 12) as i:
                plain(i)
            pe.wait_ge(ssa_sd, 1)

            def head(q, it, par):
                hc = it * 2 + (4 * q + par)

                def unit(m, k0, k1):
                    if k0 == 0:
                        if m == 0:
                            pe.wait_ge(lo_done, it * 2 + (2 * (G_O1 + 2 * q) + par + 3))
                        pe.wait_ge(ev[0], it * 4 + (C_O1 + 1 + 8 * q + 2 * par + m))
                    for k in range(k0, k1):
                        if m == 0:
                            pe.wait_ge(y_ready, k + 1)
                        mm = products(pe, m, par, k, k, YH, YL, k == 0, k == UK - 1, to=0)
                    if k1 == UK:
                        mm.then_inc(unit_done if m else m0_done, 1)

                def transposes(b, src):
                    for j in range(4):
                        t = pe.transpose(PS[:, b, 128 * j:128 * j + 128], src(j), ident[:, :])
                    t.then_inc(tp, 1)

                def score(i):
                    pe.matmul(PS[:, 2 + i % 2, 0:S_LEN[i]], QF[par][:, 128 * i:128 * i + 128], KF[par][:, 0:S_LEN[i]],
                              start=True, stop=True).then_inc(sc, 1)

                def probs_t(i):
                    n = DEC if i == 4 else 128
                    b = 6 + i % 2
                    pe.wait_ge(pn, hc * 5 + (i + 1))
                    if i < 2:
                        pe.wait_ge(tc, hc * 4 + (3 + i))
                    else:
                        pe.wait_ge(ptc, hc * 5 + (i - 1))
                    settle(pe)
                    for j in range(i + 1):
                        w = min(128, S_LEN[i] - 128 * j)
                        t = pe.transpose(PS[0:w, b, n * j:n * j + n], tile_s(i, n)[:, 128 * j:128 * j + w], ident[0:n, 0:n])
                    t.then_inc(pt, 1)

                pe.wait_ge(att_in[par], it * 80 + (160 * q + 80))
                transposes(6, lambda j: KC[:, j, :])
                transposes(7, lambda j: VF[par][:, 128 * j:128 * j + 128])
                unit(0, 0, 2)
                score(0)
                score(1)
                pe.wait_ge(tc, hc * 4 + 2)
                transposes(6, lambda j: KF[par][:, 128 * j:128 * j + 128])
                pe.transpose(PS[0:DEC, 7, 0:HD], VF[par][:, SEQ:TOK], ident[:, :])
                pe.transpose(PS[0:DEC, 7, HD:2 * HD], KF[par][:, SEQ:TOK], ident[:, :]).then_inc(tp, 1)
                unit(0, 2, 4)
                for i in range(2, 4):
                    pe.wait_ge(mx, hc * 5 + (i - 1))
                    score(i)
                pe.wait_ge(yv, hc + 1)
                pe.matmul(PS[0:DEC, 4, :], QF[par][:, SEQ:TOK], KCT[:, :], start=True, stop=True)
                pe.matmul(PS[0:DEC, 5, 0:DEC], QF[par][:, SEQ:TOK], KF[par][:, SEQ:TOK], start=True, stop=True).then_inc(sc, 1)
                unit(0, 4, 8)
                probs_t(0)
                probs_t(1)
                unit(1, 0, 3)
                probs_t(2)
                probs_t(3)
                unit(1, 3, 6)
                probs_t(4)
                unit(1, 6, 8)
                pe.wait_ge(ptc, hc * 5 + 5)
                for j in range(4):
                    pe.matmul(PS[:, 4, 128 * j:SEQ], VT[par][:, j, :], PT[:, j, 128 * j:SEQ], start=(j == 0), stop=(j == 3))
                for j in range(4):
                    pe.matmul(PS[:, 5, 0:DEC], VC[par][:, j, :], PTS[:, j, :], start=(j == 0), stop=False)
                pe.matmul(PS[:, 5, 0:DEC], VT[par][0:DEC, 4, :], PTS[0:DEC, 4, :], start=False, stop=True).then_inc(pv_done, 1)

            for q in range(2):
                with pe.Fori(0, 2) as it:
                    for par in range(2):
                        head(q, it, par)
            pe.wait_ge(last_a, 2 * (CONV - 1))
            pe.transpose(PS[0:64, 6, 0:128], last[:, :], ident[:, :]).then_inc(last_t, 1)
            pe.wait_ge(yv, 9)
            for q, n in enumerate((Q0, Q1)):
                pe.wait_ge(yss, (NH - 1) * (q + 1))
                for h in range(2):
                    mm = pe.matmul(PS[:, 2 + 2 * q + h, 0:HALF], ones[:, :], n[:, HALF * h:HALF * h + HALF], start=True, stop=True)
                mm.then_inc(y_mm, 1)
            pe.wait_ge(y_sd, 2)

            with pe.Fori(0, 4) as j:
                for s in range(2):
                    narrow(pe, j + G_O2, s, j * 2 + (C_O2 + s), YH, YL, UK, ready=y_ready, at=UK)
            pe.wait_ge(ln_sum, KT)
            for h in range(2):
                mm = pe.matmul(PS[:, 4 + h, 0:HALF], ones[:, :], NS[:, HALF * h:HALF * h + HALF], start=True, stop=True)
            mm.then_inc(ln_mm1, 1)
            for s in range(2):
                pe.wait_ge(lo_done, G_U0 * 2 + (s + 3))
                for k in range(UK):
                    kk = UK * s + k
                    pe.wait_ge(x1_ready, kk + 1)
                    for m in range(2):
                        if kk == 0:
                            pe.wait_ge(*free(m, C_U0))
                        mm = products(pe, m, s, k, kk, X1H, X1L, kk == 0, kk == KT - 1)
                        if kk == KT - 1 and m == 0:
                            mm.then_inc(m0_done, 1)
                mm.then_inc(unit_done, 1)
            for s in range(2):
                pe.wait_ge(lo_done, (G_U0 + 1) * 2 + (s + 3))
                for m in range(2):
                    if s == 0 and m == 1:
                        pe.wait_ge(ln_sd, 1)
                    for k in range(UK):
                        kk = UK * s + k
                        mm = products(pe, m, s, k, kk, X1H, X1L, kk == 0, kk == KT - 1, to=m + 2)
                        if kk == 3 and m == 0:
                            pe.wait_ge(ln_ss, KT)
                            for h in range(2):
                                var = pe.matmul(PS[:, 6 + h, 0:HALF], ones[:, :], NS[:, HALF * h:HALF * h + HALF], start=True, stop=True)
                            var.then_inc(ln_mm2, 1)
                    if m == 1:
                        mm.then_inc(unit_done, 1)
                    elif s == 1:
                        mm.then_inc(m0_done, 1)

            def up(G, C, j0=0):
                with pe.Fori(j0, 4) as j:
                    group(pe, G + j, [free(m, C + j) for m in range(2)], X1H, X1L)

            up(G_U0, C_U0, 2)
            with pe.Fori(0, 4) as j:
                for s in range(2):
                    narrow(pe, j + G_D0, s, j * 2 + (C_D0 + s), HHI, HLO, 0, ready=h_ready, at=0)
            with pe.Fori(0, MID) as c:
                up(c * 8 + G_C, c * 12 + C_C)
                with pe.Fori(0, 4) as j:
                    for s in range(2):
                        narrow(pe, c * 8 + j + (G_C + 4), s, c * 12 + j * 2 + (C_C + 4 + s), HHI, HLO, 0,
                               ready=h_ready, at=c * 8 + 8)
            up(G_U7, C_U7)

            def rows_transposed(u):
                for m in range(2):
                    pe.wait_ge(*free(m, C_D7 + u + 1))
                if u:
                    pe.wait_ge(rows_c, 3 * u)
                for t in range(TT):
                    n = min(128, TOK - 128 * t)
                    for m in range(2):
                        at = 256 * (t % 2) + 128 * m
                        tt = pe.transpose(PS[0:n, 4 + t // 2, at:at + 128], ACC[:, 2 * u + m, 128 * t:128 * t + n], ident[:, :])
                    if t % 2 or t == TT - 1:
                        tt.then_inc(rows_t, 1)

            for u in range(8):
                narrow(pe, G_D7 + u // 2, u % 2, C_D7 + u, HHI, HLO, 0,
                       ready=h_ready if u == 0 else None, at=8 * (N_CHUNK - 1))
                if u:
                    rows_transposed(u - 1)
            rows_transposed(7)


_INS = ["x_prompt", "x_sample", "state_conv", "state_lru", "cache_band_k", "cache_band_v", "cache_fox_k", "cache_fox_v",
        "cache_fox_logf", "w_in", "w_conv", "b_conv", "w_rg_a", "b_rg_a", "w_rg_x", "b_rg_x", "lru_lambda", "rel_bias",
        "b_forget", "g_mix", "w_out", "ln1_g", "ln1_b", "w_up", "w_down", "ln2_g", "ln2_b"]
_IN_SHAPES = {
    "x_prompt": (SEQ, D), "x_sample": (DEC, D), "state_conv": (CONV - 1, DA), "state_lru": (1, DA),
    "cache_band_k": (PAST, NH, HD), "cache_band_v": (PAST, NH, HD), "cache_fox_k": (PAST, NH, HD),
    "cache_fox_v": (PAST, NH, HD), "cache_fox_logf": (PAST, NH), "w_in": (D, D_IN), "w_conv": (CONV, DA),
    "b_conv": (1, DA), "w_rg_a": (NA, HD, HD), "b_rg_a": (1, DA), "w_rg_x": (NA, HD, HD), "b_rg_x": (1, DA),
    "lru_lambda": (1, DA), "rel_bias": (NH, NREL), "b_forget": (1, NH), "g_mix": (1, D), "w_out": (D, D),
    "ln1_g": (1, D), "ln1_b": (1, D), "w_up": (D, DFF), "w_down": (DFF, D), "ln2_g": (1, D), "ln2_b": (1, D)}
_OUTS = [((SEQ, D), (1, SEQ, D)), ((DEC, D), (1, DEC, D)),
         ((CONV - 1, DA), (1, 1, CONV - 1, DA)), ((1, DA), (1, 1, DA))] \
    + [((SEQ, NH, HD), (1, 1, SEQ, NH, HD))] * 4 + [((SEQ, NH), (1, 1, SEQ, NH))] \
    + [((CONV - 1, DA), (1, 1, CONV - 1, DA)), ((1, DA), (1, 1, DA))] \
    + [((DEC, NH, HD), (1, 1, DEC, NH, HD))] * 4 + [((DEC, NH), (1, 1, DEC, NH))]


def kernel(**inputs):
    import numpy as _np
    import concourse.bacc as _bacc
    from concourse.bass_utils import run_bass_kernel_spmd as _run

    nc = _bacc.Bacc("TRN2", target_bir_lowering=False, num_devices=1)
    arrays, args = {}, []
    for name in _INS:
        a = _np.ascontiguousarray(inputs[name]).reshape(_IN_SHAPES[name])
        arrays[f"in_{name}"] = a
        args.append(nc.dram_tensor(f"in_{name}", a.shape, F32, kind="ExternalInput").ap())
    for i, (shape, _) in enumerate(_OUTS):
        args.append(nc.dram_tensor(f"out_{i}", shape, F32, kind="ExternalOutput").ap())
    encoder_step(nc, *args)
    r = _run(nc, [arrays], core_ids=[0])
    return tuple(r.results[0][f"out_{i}"].reshape(full) for i, (_, full) in enumerate(_OUTS))
```
